# Optimizing a Trainium2 kernel written in Bass

```python
import jax, jax.numpy as jnp
from jax import lax
import numpy as np

D_MODEL = 2048
BATCH = 1
SEQ = 256
DEPTH = 2

CHUNK = 64
Q_BLOCK = 128
ROPE_THETA = 10000.0
EPS = 1e-6
NEG_INF = -1e30
N_BRANCH = 4
BRANCH_WIDTH = 512

A_GROUPS = 4
A_GROUP_W = 128
A_WIDTH = A_GROUPS * A_GROUP_W
A_BLOCK = 128

B_HEADS = 4
B_Q_RANK = 512
B_KV_RANK = 256
B_NOPE = 128
B_ROPE = 64
B_V = 128
B_WIDTH = B_HEADS * B_V

C_HEADS = 4
C_HEAD_DIM = 128
C_WIDTH = C_HEADS * C_HEAD_DIM
C_IDX_HEADS = 8
C_IDX_DIM = 64
C_TOPK = 256

D_HEADS = 8
D_KV_HEADS = 2
D_HEAD_DIM = 64
D_WIDTH = D_HEADS * D_HEAD_DIM
D_WINDOW = 128
D_WINDOW_CHUNKS = D_WINDOW // CHUNK

IN_SPLITS = (
    ("a_u", A_WIDTH), ("a_v", A_WIDTH), ("a_z", A_WIDTH),
    ("b_cq", B_Q_RANK), ("b_ckv", B_KV_RANK), ("b_kr", B_ROPE), ("b_z", B_WIDTH),
    ("c_q", C_WIDTH), ("c_k", C_HEAD_DIM), ("c_v", C_HEAD_DIM),
    ("c_iq", C_IDX_HEADS * C_IDX_DIM), ("c_ik", C_IDX_DIM), ("c_iw", C_IDX_HEADS), ("c_z", C_WIDTH),
    ("d_q", D_WIDTH), ("d_k", D_KV_HEADS * D_HEAD_DIM), ("d_v", D_KV_HEADS * D_HEAD_DIM), ("d_z", D_WIDTH),
    ("gate", N_BRANCH * D_MODEL),
)
IN_WIDTH = sum(w for _, w in IN_SPLITS)

kernel_name = "chunk_causal_hybrid_gated_parallel_mixers"

def rmsnorm(x, g):
    x32 = x.astype(jnp.float32)
    y = x32 * lax.rsqrt(jnp.mean(x32 * x32, axis=-1, keepdims=True) + EPS) * g.astype(jnp.float32)
    return y.astype(x.dtype)

def layernorm(x, g):
    x32 = x.astype(jnp.float32)
    mu = jnp.mean(x32, axis=-1, keepdims=True)
    xc = x32 - mu
    y = xc * lax.rsqrt(jnp.mean(xc * xc, axis=-1, keepdims=True) + EPS) * g.astype(jnp.float32)
    return y.astype(x.dtype)

def rope_tables(seq, dim):
    inv = 1.0 / (ROPE_THETA ** (jnp.arange(0, dim, 2, dtype=jnp.float32) / dim))
    ang = jnp.arange(seq, dtype=jnp.float32)[:, None] * inv[None, :]
    return jnp.cos(ang), jnp.sin(ang)

def apply_rope(x, cos, sin):
    x1, x2 = jnp.split(x.astype(jnp.float32), 2, axis=-1)
    c = cos[None, :, None, :]
    s = sin[None, :, None, :]
    return jnp.concatenate([x1 * c - x2 * s, x1 * s + x2 * c], axis=-1).astype(x.dtype)

def split_columns(proj):
    offs = np.cumsum([w for _, w in IN_SPLITS])[:-1].tolist()
    parts = jnp.split(proj, offs, axis=-1)
    return {name: p for (name, _), p in zip(IN_SPLITS, parts)}

def block_chunk_mask(q0, q1, k1):
    tq = jnp.arange(q0, q1) // CHUNK
    tk = jnp.arange(k1) // CHUNK
    return tk[None, :] <= tq[:, None]

def gmlp_branch(u, v, ln_g, w_s, b_s):
    bsz, s_len, _ = u.shape
    u = jax.nn.gelu(u)
    v = layernorm(jax.nn.gelu(v), ln_g)
    nb = s_len // A_BLOCK
    vb = v.reshape(bsz, nb, A_BLOCK, A_GROUPS, A_GROUP_W)
    pos = jnp.arange(A_BLOCK) // CHUNK
    mask = pos[None, :] <= pos[:, None]
    w = jnp.where(mask[None], w_s, 0.0).astype(v.dtype)
    mixed = jnp.einsum('gts,bnsgc->bntgc', w, vb) + b_s.T.astype(v.dtype)[None, None, :, :, None]
    return u * mixed.reshape(bsz, s_len, A_WIDTH)

def chunk_causal_attention(q, k, v, scale):
    s_len = q.shape[1]
    outs = []
    for i in range(s_len // Q_BLOCK):
        q0, q1 = i * Q_BLOCK, (i + 1) * Q_BLOCK
        sc = jnp.einsum('bthd,bshd->bhts', q[:, q0:q1], k[:, :q1]).astype(jnp.float32) * scale
        sc = jnp.where(block_chunk_mask(q0, q1, q1)[None, None], sc, NEG_INF)
        p = jax.nn.softmax(sc, axis=-1).astype(v.dtype)
        outs.append(jnp.einsum('bhts,bshd->bthd', p, v[:, :q1]))
    return jnp.concatenate(outs, axis=1)

def mla_branch(c_q, c_kv, k_r, q_norm_g, kv_norm_g, w_uq, w_ukv, cos, sin):
    bsz, s_len, _ = c_q.shape
    q = jnp.einsum('bsr,rhd->bshd', rmsnorm(c_q, q_norm_g), w_uq)
    q = jnp.concatenate([q[..., :B_NOPE], apply_rope(q[..., B_NOPE:], cos, sin)], axis=-1)
    kv = jnp.einsum('bsr,rhd->bshd', rmsnorm(c_kv, kv_norm_g), w_ukv)
    k_rope = apply_rope(k_r[:, :, None, :], cos, sin)
    k = jnp.concatenate([kv[..., :B_NOPE],
                         jnp.broadcast_to(k_rope, (bsz, s_len, B_HEADS, B_ROPE))], axis=-1)
    o = chunk_causal_attention(q, k, kv[..., B_NOPE:], (B_NOPE + B_ROPE) ** -0.5)
    return o.reshape(bsz, s_len, B_WIDTH)

def dsa_branch(q, k, v, iq, ik, iw, ik_norm_g, cos_h, sin_h, cos_i, sin_i):
    bsz, s_len, _ = q.shape
    q = apply_rope(q.reshape(bsz, s_len, C_HEADS, C_HEAD_DIM), cos_h, sin_h)
    k = apply_rope(k[:, :, None, :], cos_h, sin_h)[:, :, 0]
    iq = apply_rope(iq.reshape(bsz, s_len, C_IDX_HEADS, C_IDX_DIM), cos_i, sin_i)
    ik = apply_rope(layernorm(ik, ik_norm_g)[:, :, None, :], cos_i, sin_i)[:, :, 0]
    iw = iw.astype(jnp.float32) * (C_IDX_HEADS ** -0.5)
    n_sel = min(C_TOPK, s_len // 4)
    gather = jax.vmap(lambda arr, idx: arr[idx])
    outs = []
    for i in range(s_len // Q_BLOCK):
        q0, q1 = i * Q_BLOCK, (i + 1) * Q_BLOCK
        dots = jnp.einsum('bthd,bsd->bths', iq[:, q0:q1], ik[:, :q1]).astype(jnp.float32)
        score = jnp.einsum('bth,bths->bts', iw[:, q0:q1], jax.nn.relu(dots * C_IDX_DIM ** -0.5))
        score = jnp.where(block_chunk_mask(q0, q1, q1)[None], score, NEG_INF)
        _, idx = lax.top_k(score, min(n_sel, q1))
        ks = gather(k, idx)
        vs = gather(v, idx)
        valid = (idx // CHUNK) <= (jnp.arange(q0, q1) // CHUNK)[None, :, None]
        sc = jnp.einsum('bthd,btkd->bhtk', q[:, q0:q1], ks).astype(jnp.float32) * C_HEAD_DIM ** -0.5
        sc = jnp.where(valid[:, None], sc, NEG_INF)
        p = jax.nn.softmax(sc, axis=-1).astype(vs.dtype)
        outs.append(jnp.einsum('bhtk,btkd->bthd', p, vs))
    return jnp.concatenate(outs, axis=1).reshape(bsz, s_len, C_WIDTH)

def swa_sink_branch(q, k, v, sinks, cos, sin):
    bsz, s_len, _ = q.shape
    nc = s_len // CHUNK
    grp = D_HEADS // D_KV_HEADS
    q = apply_rope(q.reshape(bsz, s_len, D_HEADS, D_HEAD_DIM), cos, sin)
    k = apply_rope(k.reshape(bsz, s_len, D_KV_HEADS, D_HEAD_DIM), cos, sin)
    qc = q.reshape(bsz, nc, CHUNK, D_KV_HEADS, grp, D_HEAD_DIM)
    kc = k.reshape(bsz, nc, CHUNK, D_KV_HEADS, D_HEAD_DIM)
    vc = v.reshape(bsz, nc, CHUNK, D_KV_HEADS, D_HEAD_DIM)

    def band(t):
        tp = jnp.concatenate([jnp.zeros_like(t[:, :D_WINDOW_CHUNKS - 1]), t], axis=1)
        return jnp.concatenate([tp[:, j:j + nc] for j in range(D_WINDOW_CHUNKS)], axis=2)

    kb, vb = band(kc), band(vc)
    key_chunk = jnp.arange(nc)[:, None] - (D_WINDOW_CHUNKS - 1) + jnp.arange(D_WINDOW_CHUNKS)[None, :]
    valid = jnp.repeat(key_chunk >= 0, CHUNK, axis=1)
    sc = jnp.einsum('bcqkgd,bcjkd->bckgqj', qc, kb).astype(jnp.float32) * D_HEAD_DIM ** -0.5
    sc = jnp.where(valid[None, :, None, None, None, :], sc, NEG_INF)
    sink = jnp.broadcast_to(sinks.astype(jnp.float32).reshape(D_KV_HEADS, grp)[None, None, :, :, None, None],
                            sc.shape[:-1] + (1,))
    p = jax.nn.softmax(jnp.concatenate([sc, sink], axis=-1), axis=-1)[..., :-1].astype(vb.dtype)
    o = jnp.einsum('bckgqj,bcjkd->bcqkgd', p, vb)
    return o.reshape(bsz, s_len, D_WIDTH)

def hybrid_layer(x, pre_g, w_in, a_ln_g, a_w_s, a_b_s, b_q_norm_g, b_kv_norm_g, b_w_uq, b_w_ukv,
                 c_ik_norm_g, d_sinks, w_branch, w_out, post_g, rope64, rope128):
    bsz, s_len, _ = x.shape
    h = rmsnorm(x, pre_g)
    pr = split_columns(jnp.einsum('bsd,de->bse', h, w_in))
    cos64, sin64 = rope64
    cos128, sin128 = rope128
    ya = gmlp_branch(pr['a_u'], pr['a_v'], a_ln_g, a_w_s, a_b_s) * jax.nn.silu(pr['a_z'])
    yb = mla_branch(pr['b_cq'], pr['b_ckv'], pr['b_kr'], b_q_norm_g, b_kv_norm_g,
                    b_w_uq, b_w_ukv, cos64, sin64) * jax.nn.silu(pr['b_z'])
    yc = dsa_branch(pr['c_q'], pr['c_k'], pr['c_v'], pr['c_iq'], pr['c_ik'], pr['c_iw'], c_ik_norm_g,
                    cos128, sin128, cos64, sin64) * jax.nn.silu(pr['c_z'])
    yd = swa_sink_branch(pr['d_q'], pr['d_k'], pr['d_v'], d_sinks, cos64, sin64) * jax.nn.silu(pr['d_z'])
    gates = jax.nn.sigmoid(pr['gate'].reshape(bsz, s_len, N_BRANCH, D_MODEL))
    merged = None
    for b, yb_ in enumerate((ya, yb, yc, yd)):
        term = gates[:, :, b] * jnp.einsum('bsw,wd->bsd', yb_, w_branch[b])
        merged = term if merged is None else merged + term
    out = rmsnorm(jnp.einsum('bsd,de->bse', merged, w_out), post_g)
    return x + out

def setup_inputs(seed: int = 0) -> dict:
    key = jax.random.key(seed)
    ks = jax.random.split(key, 16)
    f32 = jnp.float32

    def nrm(k, shape, scale):
        return jax.random.normal(k, shape, f32) * scale

    return {
        "x": nrm(ks[0], (BATCH, SEQ, D_MODEL), 1.0),
        "pre_norm_g": 1.0 + nrm(ks[1], (DEPTH, D_MODEL), 0.02),
        "w_in": nrm(ks[2], (DEPTH, D_MODEL, IN_WIDTH), D_MODEL ** -0.5),
        "a_ln_g": 1.0 + nrm(ks[3], (DEPTH, A_WIDTH), 0.02),
        "a_w_s": nrm(ks[4], (DEPTH, A_GROUPS, A_BLOCK, A_BLOCK), A_BLOCK ** -0.5),
        "a_b_s": 1.0 + nrm(ks[5], (DEPTH, A_GROUPS, A_BLOCK), 0.02),
        "b_q_norm_g": 1.0 + nrm(ks[6], (DEPTH, B_Q_RANK), 0.02),
        "b_kv_norm_g": 1.0 + nrm(ks[7], (DEPTH, B_KV_RANK), 0.02),
        "b_w_uq": nrm(ks[8], (DEPTH, B_Q_RANK, B_HEADS, B_NOPE + B_ROPE), B_Q_RANK ** -0.5),
        "b_w_ukv": nrm(ks[9], (DEPTH, B_KV_RANK, B_HEADS, B_NOPE + B_V), B_KV_RANK ** -0.5),
        "c_ik_norm_g": 1.0 + nrm(ks[10], (DEPTH, C_IDX_DIM), 0.02),
        "d_sinks": nrm(ks[11], (DEPTH, D_HEADS), 0.5),
        "w_branch": nrm(ks[12], (DEPTH, N_BRANCH, BRANCH_WIDTH, D_MODEL), BRANCH_WIDTH ** -0.5),
        "w_out": nrm(ks[13], (DEPTH, D_MODEL, D_MODEL), D_MODEL ** -0.5),
        "post_norm_g": 1.0 + nrm(ks[14], (DEPTH, D_MODEL), 0.02),
    }

def reference(x, pre_norm_g, w_in, a_ln_g, a_w_s, a_b_s, b_q_norm_g, b_kv_norm_g, b_w_uq, b_w_ukv,
              c_ik_norm_g, d_sinks, w_branch, w_out, post_norm_g):
    s_len = x.shape[1]
    rope64 = rope_tables(s_len, 64)
    rope128 = rope_tables(s_len, 128)
    for l in range(DEPTH):
        x = hybrid_layer(x, pre_norm_g[l], w_in[l], a_ln_g[l], a_w_s[l], a_b_s[l],
                         b_q_norm_g[l], b_kv_norm_g[l], b_w_uq[l], b_w_ukv[l],
                         c_ik_norm_g[l], d_sinks[l], w_branch[l], w_out[l], post_norm_g[l],
                         rope64, rope128)
    return x


_drawn_inputs = setup_inputs


def setup_inputs(seed=0):
    import zlib

    import numpy as np

    out = dict(_drawn_inputs(seed))
    spreads = {}
    factors = {'a_ln_g': 3.243, 'a_b_s': 2.791, 'b_q_norm_g': 8.0, 'b_kv_norm_g': 6.114, 'd_sinks': 8.0}
    for name, (base, spread) in spreads.items():
        noise = np.random.default_rng([zlib.crc32(name.encode()), seed]).standard_normal(out[name].shape)
        drawn = base * np.exp(spread * noise) if base else spread * noise
        out[name] = __import__('jax').numpy.asarray(drawn.astype(out[name].dtype))
    for name, factor in factors.items():
        out[name] = (out[name] * factor).astype(out[name].dtype)
    return out
```

```python
from contextlib import ExitStack

import numpy as np

import concourse.bass as bass
from concourse import mybir

F32 = mybir.dt.float32
F32R = mybir.dt.float32r
BF16 = mybir.dt.bfloat16
I32 = mybir.dt.int32
ALU = mybir.AluOpType
ACT = mybir.ActivationFunctionType
AX_X = mybir.AxisListType.X

P = 128
DEPTH, SEQ, D_MODEL = 2, 256, 2048
TT = SEQ // P
KT = D_MODEL // P
CHUNK = 64
N_BRANCH, BW = 4, 512
BKT = BW // P
A_GROUPS = 4
B_HEADS, B_NOPE, B_ROPE, B_V = 4, 128, 64, 128
B_Q_RANK, B_KV_RANK = 512, 256
QW = B_NOPE + B_ROPE
KVW = B_NOPE + B_V
C_HEADS, C_DIM = 4, 128
I_HEADS, I_DIM = 8, 64
N_SEL = SEQ // 4
D_HEADS, D_KV, D_DIM = 8, 2, 64
EPS = 1e-6
NEG = -1e30
TAKEN = -3e38

COL = {}
_at = 0
for _name, _w in (("a_u", 512), ("a_v", 512), ("a_z", 512), ("b_cq", 512), ("b_ckv", 256), ("b_kr", 64),
                  ("b_z", 512), ("c_q", 512), ("c_k", 128), ("c_v", 128), ("c_iq", 512), ("c_ik", 64),
                  ("c_iw", 8), ("c_z", 512), ("d_q", 512), ("d_k", 128), ("d_v", 128), ("d_z", 512)):
    COL[_name] = _at
    _at += _w
MIX = _at

KC = 2
NW = 512
MG = 12
MW = MIX // MG
SLOTS = 4
CPG = KT // KC
NG = D_MODEL // NW
GATES = N_BRANCH * NG
LATENT_AT = 9
LATENT = 8
CPB = BKT // KC
CG = CPG + CPB
LATENT0 = LATENT_AT * CPG
GATE0 = MG * CPG + LATENT
OUT0 = GATE0 + GATES * CG
CHUNKS = OUT0 + NG * CPG
assert MW * MG == MIX and CHUNKS % SLOTS == 0 and LATENT0 % SLOTS == 0 and MW % 2 == 0

LAT_GROUPS = 4
DR_GATE = MG + LAT_GROUPS
DR_OUT = DR_GATE + GATES
DRAINS = DR_OUT + NG

GELU_C, GELU_S = 0.044715, float(np.sqrt(2.0 / np.pi))

PE_STEPS = ([f"hT{b}" for b in range(8)] +
            ["A1", "A2", "B1", "yA", "B3k", "B3q", "B4", "B5", "B6", "yB",
             "C1", "C2", "C3", "C4", "C5", "C6", "C7", "yC",
             "D1", "D2", "D4", "D6a", "D3", "D5", "D6b", "yD", "M0", "M1", "M2"])
ACT_STEPS = (["ss0", "h1"] + [f"hT{b}" for b in range(8)] +
             ["gelu", "zA", "B1", "zB", "yA", "B3k", "B3q", "B4", "zC", "B5", "zD", "yB",
              "C1", "C2", "C3", "C4", "C5", "C6", "yC", "D1", "D2", "D4", "D3", "D5", "yD",
              "M0", "M1", "M2"] + [f"sq{n}" for n in range(4)])
DVE_STEPS = (["start", "rs", "h0"] + [f"hT{b}" for b in range(8)] +
             ["A1", "gelu", "vn", "zA", "Bn", "A2", "B1", "yA", "zB", "B3k", "ikn", "B3q", "B4max",
              "B5", "B6", "zC", "yB", "zD", "C1", "C3", "sel0", "C4", "sel1", "C5max", "C6", "C7", "yC",
              "D1", "D2max", "D4", "D6a", "D3max", "D5", "D6b", "yD", "M0", "M1", "M2", "xn"])
POOL_STEPS = (["gelu", "kr", "q", "c", "d"] + [f"og{n}" for n in range(4)])


class Steps:

    def __init__(self, sem, names):
        self.sem, self.names, self.n = sem, names, 0

    def did(self, name):
        assert self.names[self.n] == name, (self.names[self.n], name)
        self.n += 1
        return self.sem, 1

    def at(self, layer, name):
        return layer * len(self.names) + (self.names.index(name) + 1)


def trunk(nc, x, pre_norm_g, w_in, a_ln_g, a_w_s, a_b_s, b_q_norm_g, b_kv_norm_g, b_w_uq, b_w_ukv,
          c_ik_norm_g, d_sinks, w_branch, w_out, post_norm_g, tables, masks, out):
    with ExitStack() as ctx:
        def sb(name, shape, dt=F32):
            return ctx.enter_context(nc.sbuf_tensor(name, shape, dt))

        def sem(name):
            return ctx.enter_context(nc.semaphore(name))

        wide = sb("wide", [P, TT, D_MODEL])
        area = sb("area", [P, TT, D_MODEL])
        lhs = sb("lhs", [P, 2, KT, SEQ], F32R)
        yT = sb("yT", [P, 2, 2, BKT, SEQ], F32R)
        raw = sb("raw", [P, SLOTS, KC * NW])
        w_hi = sb("w_hi", [P, SLOTS, KC * NW], F32R)
        w_lo = sb("w_lo", [P, SLOTS, KC * NW], F32R)
        proj = sb("proj", [P, TT, MIX])
        gate = sb("gate", [P, TT, NW])
        turned = sb("turned", [P, 12 * SEQ])
        tmp = sb("tmp", [P, 2, NW])
        gains = sb("gains", [P, 1352])
        tabs = sb("tabs", [P, 512])
        mask = sb("mask", [P, 3, SEQ], BF16)
        sel = sb("sel", [P, TT, SEQ], BF16)
        gcols = sb("gcols", [P, 40])
        gcol = sb("gcol", [P, KT])
        bcol = sb("bcol", [P, A_GROUPS])
        ms = sb("ms", [P, 4])
        rs = sb("rs", [P, 4])
        half = sb("half", [P, 4], I32)
        nt = sb("nt", [P, 4])
        ss = sb("ss", [P, 1])
        sq = sb("sq", [P, TT, NG])
        bn = sb("bn", [P, TT, 6])
        mv = sb("mv", [P, TT, 2])
        mx = sb("mx", [P, TT, 8])
        nmx = sb("nmx", [P, TT, 8])
        ex = sb("ex", [P, TT, 8])
        sums = sb("sums", [P, TT, 8])
        rinv = sb("rinv", [P, TT, 8])
        iw = sb("iw", [P, TT, I_HEADS])
        top = sb("top", [P, 8])
        ps = ctx.enter_context(nc.psum_tensor("ps", [P, 8, 512], F32))

        x_loaded, consts_loaded, x_stored = sem("x_loaded"), sem("consts_loaded"), sem("x_stored")
        raw_loaded = [sem(f"raw_loaded{s}") for s in range(SLOTS)]
        hi_done, lo_done, mm_done = sem("hi_done"), sem("lo_done"), sem("mm_done")
        act_drained, dve_drained = sem("act_drained"), sem("dve_drained")
        aw_loaded, gains_loaded, post_loaded, res_loaded = (sem("aw_loaded"), sem("gains_loaded"),
                                                            sem("post_loaded"), sem("res_loaded"))
        gcols_turned = sem("gcols_turned")
        dve_link, pool_link = sem("dve_link"), sem("pool_link")
        dve_waited, pool_waited = sem("dve_waited"), sem("pool_waited")
        pe_s, act_s = Steps(sem("pe_steps"), PE_STEPS), Steps(sem("act_steps"), ACT_STEPS)
        dve_s, pool_s = Steps(sem("dve_steps"), DVE_STEPS), Steps(sem("pool_steps"), POOL_STEPS)

        ident = tabs[:, 0:128]
        identb = mask[:, 0, 0:128]
        cos64 = tabs[:, 128:192].rearrange("p (t d) -> p t d", t=TT)
        sin64 = tabs[:, 192:256].rearrange("p (t d) -> p t d", t=TT)
        cos128 = tabs[:, 256:384].rearrange("p (t d) -> p t d", t=TT)
        sin128 = tabs[:, 384:512].rearrange("p (t d) -> p t d", t=TT)
        g_ln, g_q, g_kv, g_ik, sink = (gains[:, 0:512], gains[:, 512:1024], gains[:, 1024:1280],
                                       gains[:, 1280:1344], gains[:, 1344:1352])

        def part(name, w, t=slice(None)):
            return proj[:, t, COL[name]:COL[name] + w]

        gelu_arg = wide[:, :, 0:2 * BW]
        lat_q = wide[:, :, 0:B_HEADS * QW]
        lat_kv = wide[:, :, 768:768 + B_HEADS * KVW]
        a_w = wide[:, :, 1792:2048]
        q_rope = wide[:, :, 1792:2048]
        idx_score, idx_work = proj[:, :, 512:768], proj[:, :, 1024:1280]
        ik_twice, kr_twice = proj[:, :, 1280:1408], proj[:, :, 1408:1536]
        dk_twice = proj[:, :, COL["b_ckv"]:COL["b_ckv"] + 256]
        prob, probT = area[:, 0], area[:, 1]
        post_g = proj[:, 0, 0:D_MODEL]

        def rows(at, n):
            return turned[:, at * SEQ:(at + n) * SEQ].rearrange("p (k s) -> p k s", k=n)

        a_wT = rows(0, 2).rearrange("p k (h s) -> p (k h) s", h=2)
        qnT, qrT, knT, krT = rows(0, 4), rows(4, 2), rows(6, 4), rows(10, 2)
        cqT, ckT, cikT, ciqT = rows(0, 4), rows(4, 1), rows(5, 2), rows(7, 4)
        dqT, dkT = rows(0, 4), rows(4, 4)

        def bank(b, a=0, n=512):
            return ps[:, b, a:a + n]

        def wslot(buf, slot, n):
            return buf[:, slot, 0:n]

        def w_width(j):
            if LATENT0 <= j < LATENT0 + LATENT // 2:
                return KC * (B_HEADS * QW // 2)
            if LATENT0 + LATENT // 2 <= j < LATENT0 + LATENT:
                return B_HEADS * KVW // 2
            if j < GATE0:
                return KC * MW
            return KC * NW

        block = ctx.enter_context(nc.Block())

        @block.sync
        def _(sp):
            sp.dma_start(wide[:], x[0].rearrange("(t p) d -> p t d", p=P)).then_inc(x_loaded, 16)
            sp.dma_start(tabs[:], tables).then_inc(consts_loaded, 16)
            sp.dma_start(area[:, 1, 0:3 * SEQ].rearrange("p (i s) -> p i s", i=3), masks).then_inc(consts_loaded, 16)
            sp.dma_start(area[0:32, 0, 0:128], pre_norm_g.rearrange("l (k p) -> (l k) p", p=P)).then_inc(consts_loaded, 16)
            sp.dma_start(area[32:40, 0, 0:128], a_b_s.rearrange("l g p -> (l g) p")).then_inc(consts_loaded, 16)

            def load(l, j, slot, src, n):
                sp.wait_ge(lo_done, l * CHUNKS + j + 1)
                dst = wslot(raw, slot, n)
                k = src.shape[1]
                sp.dma_start(dst.rearrange("p (k n) -> p k n", k=k), src).then_inc(raw_loaded[slot], 16)

            def of(w, l, k0, nk, c0, n):
                return w[bass.ds(l, 1), k0 * P:(k0 + nk) * P, bass.ds(c0, n)].rearrange("a (k p) n -> p (a k) n", p=P)

            sp.dma_start(out[0], x[0]).then_inc(x_stored, 16)
            with nc.sync.Fori(0, DEPTH, 1) as l:
                def mix_groups(g0, n, j0):
                    with nc.sync.Fori(0, n, 1) as g:
                        for c in range(CPG):
                            load(l, j0 + c + g * CPG, c % SLOTS, of(w_in, l, KC * c, KC, g0 * MW + g * MW, MW), KC * MW)
                mix_groups(0, LATENT_AT, 0)
                j = LATENT0
                for h in range(2):
                    for c in range(2):
                        n = B_HEADS * QW // 2
                        src = b_w_uq[bass.ds(l, 1), KC * c * P:KC * (c + 1) * P].rearrange(
                            "a (k p) h d -> p (a k) (h d)", p=P)[:, :, h * n:(h + 1) * n]
                        load(l, j, j % SLOTS, src, KC * n)
                        j += 1
                for h in range(2):
                    for c in range(2):
                        n = B_HEADS * KVW // 2
                        src = b_w_ukv[bass.ds(l, 1), c * P:(c + 1) * P].rearrange(
                            "a p h d -> p a (h d)")[:, :, h * n:(h + 1) * n]
                        load(l, j, j % SLOTS, src, n)
                        j += 1
                mix_groups(LATENT_AT, MG - LATENT_AT, LATENT0 + LATENT)
                with nc.sync.Fori(0, GATES // 2, 1) as g2:
                    for h in range(2):
                        for c in range(CG):
                            j = GATE0 + h * CG + c + g2 * (2 * CG)
                            if c < CPG:
                                src = of(w_in, l, KC * c, KC, g2 * (2 * NW) + (MIX + h * NW), NW)
                            else:
                                k0 = KC * (c - CPG)
                                src = w_branch[bass.ds(l, 1), bass.ds(g2 // 2, 1), k0 * P:(k0 + KC) * P,
                                               bass.ds((g2 % 2) * (2 * NW) + h * NW, NW)].rearrange(
                                    "a b (k p) n -> p (a b k) n", p=P)
                            load(l, j, (GATE0 + h * CG + c) % SLOTS, src, KC * NW)
                sp.wait_ge(dve_s.sem, dve_s.at(l, "yD"))
                sp.wait_ge(x_stored, l * 16 + 16)
                sp.dma_start(area[:], out[0].rearrange("(t p) d -> p t d", p=P)).then_inc(res_loaded, 16)
                with nc.sync.Fori(0, NG, 1) as g:
                    for c in range(CPG):
                        load(l, OUT0 + c + g * CPG, c % SLOTS, of(w_out, l, KC * c, KC, g * NW, NW), KC * NW)
                sp.wait_ge(dve_s.sem, dve_s.at(l, "xn"))
                sp.dma_start(out[0].rearrange("(t p) d -> p t d", p=P), wide[:]).then_inc(x_stored, 16)
            sp.wait_ge(x_stored, (DEPTH + 1) * 16)

        @block.gpsimd
        def _(pool):
            links = [0]
            POOL_LINKS = 30

            def link(ins):
                links[0] += 1
                ins.then_inc(pool_link, 1)
                pool.wait_ge(pool_link, l * POOL_LINKS + links[0])

            def rope(dst, src, cos, sin, t, heads, d, copies=1, step=None):
                def halves(ap):
                    return ap.rearrange("p (h e d) -> p h e d", h=heads, e=2)
                hd = d // 2
                a = tmp[:, 0, 0:heads * d].rearrange("p (h e d) -> p h e d", h=heads, e=2)
                b = tmp[:, 1, 0:heads * d].rearrange("p (h e d) -> p h e d", h=heads, e=2)
                c4 = cos[:, t].unsqueeze(1).unsqueeze(1).to_broadcast([P, heads, 2, hd])
                s3 = sin[:, t].unsqueeze(1).to_broadcast([P, heads, hd])
                pool.tensor_tensor(a, src, c4, ALU.mult)
                pool.tensor_tensor(b[:, :, 0], src[:, :, 1], s3, ALU.mult)
                link(pool.tensor_tensor(b[:, :, 1], src[:, :, 0], s3, ALU.mult))
                for i in range(copies):
                    pool.tensor_tensor(dst[i][:, :, 0], a[:, :, 0], b[:, :, 0], ALU.subtract)
                    last = pool.tensor_tensor(dst[i][:, :, 1], a[:, :, 1], b[:, :, 1], ALU.add)
                return last

            def split_heads(ap, heads):
                return ap.rearrange("p (h e d) -> p h e d", h=heads, e=2)

            pool.memset(tmp[:], 0.0).then_inc(lo_done, SLOTS)
            pool.wait_ge(consts_loaded, 64)
            with nc.gpsimd.Fori(0, DEPTH, 1) as l:
                pool.wait_ge(dve_s.sem, dve_s.at(l, "h0"))
                pool.wait_ge(act_s.sem, act_s.at(l, "h1"))
                pool.wait_ge(x_stored, l * 16 + 16)
                for t in range(TT):
                    pool.dma_start(a_w[:, t].rearrange("p (g s) -> p g s", g=2),
                                   a_w_s[bass.ds(l, 1), 2 * t:2 * t + 2].rearrange("a g t s -> t (a g) s")).then_inc(aw_loaded, 16)
                for dst, src in ((g_ln, a_ln_g), (g_q, b_q_norm_g), (g_kv, b_kv_norm_g), (g_ik, c_ik_norm_g), (sink, d_sinks)):
                    pool.dma_start(dst, src[bass.ds(l, 1)].to_broadcast([P, src.shape[1]])).then_inc(gains_loaded, 16)
                pool.wait_ge(act_drained, l * DRAINS + 4)
                pool.wait_ge(dve_drained, l * DRAINS + 4)
                uv = proj[:, :, 0:2 * BW]
                link(pool.tensor_tensor(gelu_arg, uv, uv, ALU.mult))
                pool.sem_inc(pool_waited, 1)
                link(pool.tensor_scalar(gelu_arg, gelu_arg, GELU_C, 1.0, ALU.mult, ALU.add))
                pool.tensor_tensor(gelu_arg, gelu_arg, uv, ALU.mult).then_inc(*pool_s.did("gelu"))
                pool.wait_ge(dve_s.sem, dve_s.at(l, "A2"))
                for t in range(TT):
                    kr = split_heads(part("b_kr", B_ROPE, t), 1)
                    last = rope([split_heads(kr_twice[:, t, i * 64:(i + 1) * 64], 1) for i in range(2)],
                                kr, cos64, sin64, t, 1, B_ROPE, copies=2)
                    if t + 1 < TT:
                        link(last)
                last.then_inc(*pool_s.did("kr"))
                pool.wait_ge(pool_s.sem, pool_s.at(l, "kr"))
                pool.wait_ge(act_drained, l * DRAINS + LATENT_AT + 2)
                pool.wait_ge(dve_drained, l * DRAINS + LATENT_AT + 2)
                for t in range(TT):
                    src = lat_q[:, t].rearrange("p (h w) -> p h w", h=B_HEADS)[:, :, B_NOPE:QW].rearrange(
                        "p h (e d) -> p h e d", e=2)
                    last = rope([split_heads(q_rope[:, t], B_HEADS)], src, cos64, sin64, t, B_HEADS, B_ROPE)
                    if t + 1 < TT:
                        link(last)
                last.then_inc(*pool_s.did("q"))
                pool.wait_ge(pool_s.sem, pool_s.at(l, "q"))
                pool.wait_ge(act_drained, l * DRAINS + 14)
                pool.wait_ge(dve_drained, l * DRAINS + 14)
                pool.wait_ge(dve_s.sem, dve_s.at(l, "ikn"))
                for t in range(TT):
                    for name, heads, d, co, si in (("c_q", C_HEADS, C_DIM, cos128, sin128), ("c_k", 1, C_DIM, cos128, sin128),
                                                   ("c_iq", I_HEADS, I_DIM, cos64, sin64)):
                        v = split_heads(part(name, heads * d, t), heads)
                        link(rope([v], v, co, si, t, heads, d))
                    v = split_heads(part("c_ik", I_DIM, t), 1)
                    last = rope([split_heads(ik_twice[:, t, i * 64:(i + 1) * 64], 1) for i in range(2)],
                                v, cos64, sin64, t, 1, I_DIM, copies=2)
                    if t + 1 < TT:
                        link(last)
                last.then_inc(*pool_s.did("c"))
                pool.wait_ge(pool_s.sem, pool_s.at(l, "c"))
                pool.wait_ge(act_drained, l * DRAINS + DR_GATE)
                pool.wait_ge(dve_drained, l * DRAINS + DR_GATE)
                for t in range(TT):
                    v = split_heads(part("d_q", D_HEADS * D_DIM, t), D_HEADS)
                    link(rope([v], v, cos64, sin64, t, D_HEADS, D_DIM))
                    v = split_heads(part("d_k", D_KV * D_DIM, t), D_KV)
                    twice = dk_twice[:, t].rearrange("p (h i e d) -> p i h e d", h=D_KV, i=2, e=2)
                    last = rope([twice[:, 0], twice[:, 1]], v, cos64, sin64, t, D_KV, D_DIM, copies=2)
                    if t + 1 < TT:
                        link(last)
                last.then_inc(*pool_s.did("d"))
                pool.wait_ge(dve_s.sem, dve_s.at(l, "yD"))
                pool.dma_start(post_g, post_norm_g[bass.ds(l, 1)].to_broadcast([P, D_MODEL])).then_inc(post_loaded, 16)
                pool.wait_ge(post_loaded, l * 16 + 16)
                for n in range(NG):
                    pool.wait_ge(act_s.sem, act_s.at(l, f"sq{n}"))
                    cols = wide[:, :, n * NW:(n + 1) * NW]
                    pool.tensor_tensor(cols, cols, post_g[:, n * NW:(n + 1) * NW].unsqueeze(1).to_broadcast([P, TT, NW]),
                                       ALU.mult).then_inc(*pool_s.did(f"og{n}"))
            assert links[0] == POOL_LINKS, links[0]

        @block.scalar
        def _(act):

            def split(l, j, jn=None):
                jn = j if jn is None else jn
                n, s = w_width(jn), jn % SLOTS
                act.wait_ge(raw_loaded[s], (l * CHUNKS + (j - s)) * (16 // SLOTS) + 16)
                act.wait_ge(mm_done, l * CHUNKS + j + 1)
                act.activation(wslot(w_hi, s, n), wslot(raw, s, n), ACT.Copy).then_inc(hi_done, 1)

            def splits(l, a, b):
                for j in range(a, b):
                    split(l, j)

            def drain(l, q, dst, seen, func=ACT.Copy):
                act.wait_ge(mm_done, l * CHUNKS + seen + 1 + SLOTS)
                act.activation(dst, bank((q % 2) * 2, 0, dst.shape[-1]), func).then_inc(act_drained, 1)

            def turned_hi(l, name, b, dst, scale=1.0, last=True):
                act.wait_ge(pe_s.sem, pe_s.at(l, name))
                ins = act.activation(dst, bank(b), ACT.Copy, scale=scale)
                if last:
                    ins.then_inc(*act_s.did(name))

            def softmax(t, heads, b0, at, scale):
                width = P * (t + 1)
                per = 512 // width
                for h in range(heads):
                    last = act.activation(prob[:, at + h * width:at + (h + 1) * width],
                                          bank(b0 + h // per, (h % per) * width, width), ACT.Exp,
                                          bias=nmx[:, t, h:h + 1], scale=scale, accum_out=sums[:, t, h:h + 1])
                return last

            def half_tanh(name, part_name):
                act.activation(gate[:], part(part_name, BW), ACT.Tanh, scale=0.5).then_inc(*act_s.did(name))

            def evac(dst, b, a=0, n=512):
                return act.activation(dst, bank(b, a, n), ACT.Copy)

            with nc.scalar.Fori(0, DEPTH, 1) as l:
                act.wait_ge(dve_s.sem, dve_s.at(l, "start"))
                act.activation(area[:, 0], wide[:, 0], ACT.Square, accum_out=ss[:]).then_inc(*act_s.did("ss0"))
                splits(l, 0, 2)
                act.wait_ge(dve_s.sem, dve_s.at(l, "rs"))
                act.activation(area[:, 1], wide[:, 1], ACT.Copy, scale=rs[:, 1:2]).then_inc(*act_s.did("h1"))
                for b in range(8):
                    act.wait_ge(pe_s.sem, pe_s.at(l, f"hT{b}"))
                    for i in range(2):
                        k = 2 * b + i
                        last = act.activation(lhs[:, 0, k], bank(b, i * SEQ, SEQ), ACT.Copy, scale=gcol[:, k:k + 1])
                    last.then_inc(*act_s.did(f"hT{b}"))
                splits(l, 2, 8)

                def mix_group(g, q, gn, j0, jn):
                    for c in range(4):
                        split(l, j0 + c, jn + c)
                    drain(l, q - 1, proj[:, 0, bass.ds((g - 1) * MW, MW)], j0 - 1)
                    for c in range(4, CPG):
                        split(l, j0 + c, jn + c)

                with nc.scalar.Fori(0, 2, 1) as i:
                    for h in range(2):
                        j0 = (1 + h) * CPG
                        for c in range(4):
                            split(l, i * (2 * CPG) + (j0 + c), j0 + c)
                        act.wait_ge(mm_done, (l * CHUNKS + (j0 + SLOTS)) + i * (2 * CPG))
                        act.activation(proj[:, 0, bass.ds(i * (2 * MW) + h * MW, MW)], bank(h * 2, 0, MW), ACT.Copy).then_inc(act_drained, 1)
                        for c in range(4, CPG):
                            split(l, i * (2 * CPG) + (j0 + c), j0 + c)

                def col(g):
                    return proj[:, 0, g * MW:(g + 1) * MW]
                j = 5 * CPG
                splits(l, j, j + 4)
                drain(l, 4, col(4), j - 1)
                splits(l, j + 4, j + 5)
                act.wait_ge(pool_s.sem, pool_s.at(l, "gelu"))
                act.activation(gelu_arg, gelu_arg, ACT.Tanh, scale=GELU_S).then_inc(*act_s.did("gelu"))
                splits(l, j + 5, j + 8)
                half_tanh("zA", "a_z")
                for g in (6, 7, 8):
                    j = g * CPG
                    splits(l, j, j + 4)
                    drain(l, g - 1, col(g - 1), j - 1)
                    splits(l, j + 4, j + 5)
                    if g == 8:
                        turned_hi(l, "B1", 6, yT[:, 0, 0, 0:2].rearrange("p k s -> p (k s)"), last=False)
                        turned_hi(l, "B1", 7, yT[:, 0, 0, 2:4].rearrange("p k s -> p (k s)"), last=False)
                        turned_hi(l, "B1", 4, yT[:, 1, 0, 0:2].rearrange("p k s -> p (k s)"))
                    splits(l, j + 5, j + 8)
                act.wait_ge(dve_s.sem, dve_s.at(l, "Bn"))
                half_tanh("zB", "b_z")
                j = LATENT0
                n = B_HEADS * QW // 2
                splits(l, j, j + 4)
                drain(l, 8, col(8), j - 1)
                splits(l, j + 4, j + 6)
                drain(l, 9, lat_q[:, 0, 0:n], j + 1)
                splits(l, j + 6, j + 8)
                drain(l, 10, lat_q[:, 0, n:2 * n], j + 3)
                j = LATENT0 + LATENT
                splits(l, j, j + 2)
                drain(l, 11, lat_kv[:, 0, 0:512], j - 3)
                splits(l, j + 2, j + 4)
                drain(l, 12, lat_kv[:, 0, 512:1024], j - 1)
                splits(l, j + 4, j + 5)
                for i in range(2):
                    turned_hi(l, "yA", 4 + i, yT[:, 0, 0, 2 * i:2 * i + 2].rearrange("p k s -> p (k s)"), 0.125, last=(i == 1))
                splits(l, j + 5, j + 8)
                j += CPG
                splits(l, j, j + 4)
                drain(l, 13, col(9), j - 1)
                splits(l, j + 4, j + 5)
                act.wait_ge(pe_s.sem, pe_s.at(l, "B3k"))
                evac(knT[:, 0:2].rearrange("p k s -> p (k s)"), 6)
                for r in range(2):
                    last = act.activation(krT[r * 64:(r + 1) * 64, r], ps[r * 64:(r + 1) * 64, 4, 0:SEQ], ACT.Copy)
                last.then_inc(*act_s.did("B3k"))
                splits(l, j + 5, j + 8)
                j += CPG
                splits(l, j, j + 1)
                act.wait_ge(pe_s.sem, pe_s.at(l, "B3q"))
                evac(qnT[:, 0:2].rearrange("p k s -> p (k s)"), 5)
                evac(qrT[:].rearrange("p k s -> p (k s)"), 7).then_inc(*act_s.did("B3q"))
                splits(l, j + 1, j + 4)
                drain(l, 14, col(10), j - 1)
                splits(l, j + 4, j + 5)
                act.wait_ge(dve_s.sem, dve_s.at(l, "B4max"))
                softmax(0, B_HEADS, 4, 0, QW ** -0.5)
                softmax(1, B_HEADS, 5, 512, QW ** -0.5).then_inc(*act_s.did("B4"))
                splits(l, j + 5, j + 8)
                act.wait_ge(dve_s.sem, dve_s.at(l, "zB"))
                half_tanh("zC", "c_z")

                for G in range(GATES):
                    j = GATE0 + G * CG
                    splits(l, j, j + 1)
                    if G == 0:
                        act.wait_ge(pe_s.sem, pe_s.at(l, "B5"))
                        evac(probT[:, 0:512], 4)
                        evac(probT[:, 1024:1536], 6).then_inc(*act_s.did("B5"))
                    splits(l, j + 1, j + 2)
                    if G > 0:
                        act.wait_ge(mm_done, l * CHUNKS + (j - 3) + 1 + SLOTS)
                        if G == 1:
                            act.wait_ge(dve_s.sem, dve_s.at(l, "zD"))
                        else:
                            act.wait_ge(dve_drained, l * DRAINS + DR_GATE + G - 1)
                        for t in range(TT):
                            last = act.activation(gate[:, t], bank(t), ACT.Tanh, scale=0.5)
                        last.then_inc(act_drained, 1)
                    splits(l, j + 2, j + 4)
                    if G == 0:
                        drain(l, 15, col(11), j - 1)
                    splits(l, j + 4, j + 5)
                    if G == 1:
                        act.wait_ge(pe_s.sem, pe_s.at(l, "C1"))
                        evac(cqT[:, 0:2].rearrange("p k s -> p (k s)"), 4)
                        evac(ciqT[:, 0:2].rearrange("p k s -> p (k s)"), 6).then_inc(*act_s.did("C1"))
                    if G == 2:
                        act.wait_ge(pe_s.sem, pe_s.at(l, "C3"))
                        act.activation(probT[:, 0:512], bank(4), ACT.Relu, scale=I_DIM ** -0.5)
                        act.activation(probT[:, 512:1024], bank(5), ACT.Relu, scale=I_DIM ** -0.5).then_inc(*act_s.did("C3"))
                    if G == 4:
                        act.wait_ge(dve_s.sem, dve_s.at(l, "C5max"))
                        softmax(0, C_HEADS, 4, 0, C_DIM ** -0.5)
                        softmax(1, C_HEADS, 5, 512, C_DIM ** -0.5).then_inc(*act_s.did("C5"))
                    if G == 6:
                        act.wait_ge(pe_s.sem, pe_s.at(l, "D1"))
                        evac(dqT[:, 0:2].rearrange("p k s -> p (k s)"), 4).then_inc(*act_s.did("D1"))
                    if G == 7:
                        act.wait_ge(pe_s.sem, pe_s.at(l, "D4"))
                        evac(probT[:, 0:512], 4).then_inc(*act_s.did("D4"))
                    if G == 8:
                        act.wait_ge(dve_s.sem, dve_s.at(l, "D3max"))
                        act.activation(ex[:, 1], ex[:, 1], ACT.Exp)
                        softmax(1, D_HEADS, 4, 0, D_DIM ** -0.5).then_inc(*act_s.did("D3"))
                    splits(l, j + 5, j + 8)
                    if G == 0:
                        act.wait_ge(dve_s.sem, dve_s.at(l, "zC"))
                        half_tanh("zD", "d_z")
                    splits(l, j + 8, j + 10)
                    if G in (0, 5, 9):
                        name, buf, b0 = {0: ("yB", 1, 4), 5: ("yC", 0, 4), 9: ("yD", 1, 4)}[G]
                        for i in range(2):
                            turned_hi(l, name, b0 + i, yT[:, buf, 0, 2 * i:2 * i + 2].rearrange("p k s -> p (k s)"), 0.25, last=(i == 1))
                    if G == 1:
                        act.wait_ge(pe_s.sem, pe_s.at(l, "C2"))
                        evac(ckT[:, 0], 4, 0, SEQ)
                        for r in range(2):
                            last = act.activation(cikT[r * 64:(r + 1) * 64, r], ps[r * 64:(r + 1) * 64, 4, SEQ:2 * SEQ], ACT.Copy)
                        last.then_inc(*act_s.did("C2"))
                    if G == 2:
                        act.wait_ge(pe_s.sem, pe_s.at(l, "C4"))
                        act.wait_ge(dve_s.sem, dve_s.at(l, "C3"))
                        for b in range(4):
                            last = act.activation(probT[:, b * 512:(b + 1) * 512], bank(4 + b), ACT.Relu, scale=I_DIM ** -0.5)
                        last.then_inc(*act_s.did("C4"))
                    if G == 4:
                        act.wait_ge(pe_s.sem, pe_s.at(l, "C6"))
                        evac(probT[:, 0:512], 4)
                        evac(probT[:, 1024:1536], 6).then_inc(*act_s.did("C6"))
                    if G == 6:
                        act.wait_ge(dve_s.sem, dve_s.at(l, "D2max"))
                        act.activation(ex[:, 0], ex[:, 0], ACT.Exp)
                        softmax(0, D_HEADS, 4, 0, D_DIM ** -0.5).then_inc(*act_s.did("D2"))
                    if G == 8:
                        act.wait_ge(pe_s.sem, pe_s.at(l, "D5"))
                        for b in range(2):
                            last = evac(probT[:, b * 512:(b + 1) * 512], 4 + b)
                        last.then_inc(*act_s.did("D5"))
                    if G == GATES - 1:
                        for i in range(4):
                            turned_hi(l, "M0", 4 + i, lhs[:, 0, 2 * i:2 * i + 2].rearrange("p k s -> p (k s)"), last=(i == 3))
                j = OUT0
                act.wait_ge(mm_done, l * CHUNKS + (j - 3) + 1 + SLOTS)
                act.wait_ge(dve_drained, l * DRAINS + DR_OUT - 1)
                for t in range(TT):
                    last = act.activation(gate[:, t], bank(t), ACT.Tanh, scale=0.5)
                last.then_inc(act_drained, 1)
                splits(l, j, j + 2)
                for i in range(2):
                    turned_hi(l, "M1", 4 + i, lhs[:, 0, 8 + 2 * i:10 + 2 * i].rearrange("p k s -> p (k s)"), last=(i == 1))
                splits(l, j + 2, j + 4)
                for i in range(2):
                    turned_hi(l, "M2", 6 + i, lhs[:, 0, 12 + 2 * i:14 + 2 * i].rearrange("p k s -> p (k s)"), last=(i == 1))
                splits(l, j + 4, j + 8)

                def out_drain(n):
                    act.wait_ge(mm_done, l * CHUNKS + OUT0 + (n + 1) * CPG + SLOTS)
                    act.activation(wide[:, 0, n * NW:(n + 1) * NW], bank((n % 2) * 2), ACT.Copy).then_inc(act_drained, 1)
                    act.wait_ge(act_drained, l * DRAINS + DR_OUT + n + 1)
                    act.activation(gate[:, 0], wide[:, 0, n * NW:(n + 1) * NW], ACT.Square, accum_out=sq[:, 0, n:n + 1])
                    act.wait_ge(dve_drained, l * DRAINS + DR_OUT + n + 1)
                    act.activation(gate[:, 1], wide[:, 1, n * NW:(n + 1) * NW], ACT.Square,
                                   accum_out=sq[:, 1, n:n + 1]).then_inc(*act_s.did(f"sq{n}"))

                for n in range(1, NG):
                    j = OUT0 + n * CPG
                    splits(l, j, j + 4)
                    out_drain(n - 1)
                    splits(l, j + 4, j + 8)
                out_drain(NG - 1)
                assert act_s.n == len(ACT_STEPS)

        @block.vector
        def _(dve):
            links = [0]
            DVE_LINKS = 182

            def link(ins):
                links[0] += 1
                ins.then_inc(dve_link, 1)
                dve.wait_ge(dve_link, l * DVE_LINKS + links[0])

            def own_wait():
                dve.sem_inc(dve_waited, 1)

            def split(l, j, jn=None):
                jn = j if jn is None else jn
                n, s = w_width(jn), jn % SLOTS
                dve.wait_ge(hi_done, l * CHUNKS + j + 1)
                dve.tensor_tensor(wslot(w_lo, s, n), wslot(raw, s, n), wslot(w_hi, s, n).bitcast(F32),
                                  ALU.subtract).then_inc(lo_done, 1)

            def splits(l, a, b):
                for j in range(a, b):
                    split(l, j)

            def drain(l, q, dst, seen):
                dve.wait_ge(mm_done, l * CHUNKS + seen + 1 + SLOTS)
                dve.tensor_copy(dst, bank((q % 2) * 2 + 1, 0, dst.shape[-1])).then_inc(dve_drained, 1)

            def rsqrt(n):
                v, y, a = ms[:, 0:n], rs[:, 0:n], nt[:, 0:n]
                link(dve.tensor_scalar(half[:, 0:n], v.bitcast(I32), 1, None, ALU.logical_shift_right))
                link(dve.tensor_scalar(y.bitcast(I32), half[:, 0:n], -1.0, float(0x5f3759df), ALU.mult, ALU.add))
                for i in range(4):
                    link(dve.tensor_tensor(a, y, y, ALU.mult))
                    link(dve.tensor_tensor(a, a, v, ALU.mult))
                    link(dve.tensor_scalar(a, a, -0.5, 1.5, ALU.mult, ALU.add))
                    last = dve.tensor_tensor(y, y, a, ALU.mult)
                    if i < 3:
                        link(last)
                return last

            def mean_square(dst, v, n):
                return dve.tensor_tensor_reduce(gate[:, 0, 0:n] if n <= NW else area[:, 1], v, v, 1.0 / n, EPS,
                                                ALU.mult, ALU.add, dst)

            def turned_lo(l, name, b, dst, hi, scale=1.0, last=True):
                ins = dve.scalar_tensor_tensor(out=dst, in0=bank(b), scalar=scale, in1=hi.bitcast(F32),
                                               op0=ALU.mult, op1=ALU.subtract)
                if last:
                    ins.then_inc(*dve_s.did(name))

            def both(buf, i, k):
                return (buf[:, i, k:k + 2].rearrange("p k s -> p (k s)"))

            def y_turned(name, buf, scale):
                dve.wait_ge(act_s.sem, act_s.at(l, name))
                for i in range(2):
                    turned_lo(l, name, 4 + i, both(yT[:, buf], 1, 2 * i), both(yT[:, buf], 0, 2 * i), scale, last=(i == 1))

            def times_silu(name, part_name):
                dve.wait_ge(act_s.sem, act_s.at(l, name))
                z = part(part_name, BW)
                dve.scalar_tensor_tensor(out=z, in0=gate[:], scalar=1.0, in1=z, op0=ALU.add, op1=ALU.mult).then_inc(*dve_s.did(name))

            def zero_others(tiles):
                for r in range(2):
                    dve.memset(tiles[(1 - r) * 64:(2 - r) * 64, r], 0.0)

            def row_max(l, t, heads, width, b0):
                per = 512 // width
                for b in range(heads // per):
                    last = dve.tensor_reduce(mx[:, t, b * per:(b + 1) * per],
                                             bank(b0 + b).rearrange("p (h s) -> p h s", h=per), AX_X, ALU.max)
                return last

            def attended(name, dst, z, b0, heads, ts):
                dve.wait_ge(pe_s.sem, pe_s.at(l, name))
                for i, t in enumerate(ts):
                    r = rinv[:, t, 0:heads].unsqueeze(2).to_broadcast([P, heads, BW // heads])
                    link(dve.tensor_tensor(dst[:, t].rearrange("p (h d) -> p h d", h=heads),
                                           bank(b0 + i).rearrange("p (h d) -> p h d", h=heads), r, ALU.mult))
                    last = dve.tensor_tensor(dst[:, t], dst[:, t], z[:, t], ALU.mult)
                last.then_inc(*dve_s.did(name))

            def col(g):
                return proj[:, 1, g * MW:(g + 1) * MW]

            dve.memset(top[:], 0.0).then_inc(mm_done, SLOTS)
            dve.wait_ge(consts_loaded, 64)
            dve.tensor_copy(mask[:].rearrange("p i s -> p (i s)"), area[:, 1, 0:3 * SEQ])
            dve.wait_ge(gcols_turned, 1)
            dve.tensor_copy(gcols[:], bank(0, 0, 40)).then_inc(gcols_turned, 1)
            dve.wait_ge(gcols_turned, 2)
            dve.wait_ge(x_loaded, 16)

            with nc.vector.Fori(0, DEPTH, 1) as l:
                dve.tensor_copy(gcol[:], gcols[:, bass.ds(l * KT, KT)])
                dve.tensor_copy(bcol[:], gcols[:, bass.ds(l * A_GROUPS + DEPTH * KT, A_GROUPS)]).then_inc(*dve_s.did("start"))
                mean_square(ms[:, 1:2], wide[:, 1], D_MODEL)
                dve.wait_ge(act_s.sem, act_s.at(l, "ss0"))
                link(dve.tensor_scalar(ms[:, 0:1], ss[:], 1.0 / D_MODEL, EPS, ALU.mult, ALU.add))
                rsqrt(2).then_inc(*dve_s.did("rs"))
                dve.wait_ge(dve_s.sem, dve_s.at(l, "rs"))
                dve.tensor_scalar(area[:, 0], wide[:, 0], rs[:, 0:1], None, ALU.mult).then_inc(*dve_s.did("h0"))
                splits(l, 0, 2)
                for b in range(8):
                    dve.wait_ge(act_s.sem, act_s.at(l, f"hT{b}"))
                    for i in range(2):
                        k = 2 * b + i
                        last = dve.scalar_tensor_tensor(out=lhs[:, 1, k], in0=bank(b, i * SEQ, SEQ), scalar=gcol[:, k:k + 1],
                                                        in1=lhs[:, 0, k].bitcast(F32), op0=ALU.mult, op1=ALU.subtract)
                    last.then_inc(*dve_s.did(f"hT{b}"))
                splits(l, 2, 8)
                with nc.vector.Fori(0, 2, 1) as i:
                    for h in range(2):
                        j0 = (1 + h) * CPG
                        for c in range(4):
                            split(l, i * (2 * CPG) + (j0 + c), j0 + c)
                        dve.wait_ge(mm_done, (l * CHUNKS + (j0 + SLOTS)) + i * (2 * CPG))
                        dve.tensor_copy(proj[:, 1, bass.ds(i * (2 * MW) + h * MW, MW)], bank(h * 2 + 1, 0, MW)).then_inc(dve_drained, 1)
                        for c in range(4, CPG):
                            split(l, i * (2 * CPG) + (j0 + c), j0 + c)
                j = 5 * CPG
                splits(l, j, j + 4)
                drain(l, 4, col(4), j - 1)
                splits(l, j + 4, j + 5)
                dve.wait_ge(pe_s.sem, pe_s.at(l, "A1"))
                wt = bank(4).rearrange("p (g s) -> p g s", g=A_GROUPS)
                dve.tensor_copy(a_wT[0:64], wt[0:64])
                dve.memset(a_wT[64:128, :, 0:64], 0.0)
                dve.tensor_copy(a_wT[64:128, :, 64:128], wt[64:128, :, 64:128]).then_inc(*dve_s.did("A1"))
                splits(l, j + 5, j + 8)
                j = 6 * CPG
                splits(l, j, j + 1)
                dve.wait_ge(act_s.sem, act_s.at(l, "gelu"))
                u, v = part("a_u", BW), part("a_v", BW)
                dve.scalar_tensor_tensor(out=u, in0=gelu_arg[:, :, 0:BW], scalar=1.0, in1=u, op0=ALU.add, op1=ALU.mult)
                link(dve.scalar_tensor_tensor(out=v, in0=gelu_arg[:, :, BW:2 * BW], scalar=1.0, in1=v, op0=ALU.add, op1=ALU.mult))
                for t in range(TT):
                    last = dve.bn_stats(bn[:, t], v[:, t])
                last.then_inc(*dve_s.did("gelu"))
                splits(l, j + 1, j + 4)
                drain(l, 5, col(5), j - 1)
                splits(l, j + 4, j + 5)
                dve.wait_ge(dve_s.sem, dve_s.at(l, "gelu"))
                own_wait()
                for t in range(TT):
                    last = dve.bn_aggr(mv[:, t], bn[:, t])
                link(last)
                link(dve.tensor_scalar(ms[:, 0:2], mv[:, :, 1], 0.25, EPS, ALU.mult, ALU.add))
                link(rsqrt(2))
                link(dve.tensor_scalar(rs[:, 0:2], rs[:, 0:2], 0.5, None, ALU.mult))
                for t in range(TT):
                    last = dve.tensor_scalar(v[:, t], v[:, t], mv[:, t, 0:1], rs[:, t:t + 1], ALU.subtract, ALU.mult)
                link(last)
                dve.wait_ge(gains_loaded, l * 80 + 80)
                dve.tensor_tensor(v, v, g_ln.unsqueeze(1).to_broadcast([P, TT, BW]), ALU.mult).then_inc(*dve_s.did("vn"))
                splits(l, j + 5, j + 8)
                times_silu("zA", "a_z")
                j = 7 * CPG
                splits(l, j, j + 1)
                dve.wait_ge(dve_s.sem, dve_s.at(l, "zA"))
                cq, ckv = part("b_cq", BW), part("b_ckv", B_KV_RANK)
                dve.wait_ge(act_drained, l * DRAINS + 5)
                for t in range(TT):
                    link(mean_square(ms[:, t:t + 1], cq[:, t], B_Q_RANK))
                    link(mean_square(ms[:, 2 + t:3 + t], ckv[:, t], B_KV_RANK))
                link(rsqrt(4))
                for t in range(TT):
                    dve.scalar_tensor_tensor(out=cq[:, t], in0=cq[:, t], scalar=rs[:, t:t + 1], in1=g_q, op0=ALU.mult, op1=ALU.mult)
                    last = dve.scalar_tensor_tensor(out=ckv[:, t], in0=ckv[:, t], scalar=rs[:, 2 + t:3 + t], in1=g_kv, op0=ALU.mult, op1=ALU.mult)
                last.then_inc(*dve_s.did("Bn"))
                splits(l, j + 1, j + 4)
                drain(l, 6, col(6), j - 1)
                splits(l, j + 4, j + 5)
                dve.wait_ge(pe_s.sem, pe_s.at(l, "A2"))
                bb = bcol[:].unsqueeze(2).to_broadcast([P, A_GROUPS, P])
                for t in range(TT):
                    link(dve.tensor_tensor(v[:, t].rearrange("p (g s) -> p g s", g=A_GROUPS),
                                           bank(4 + t).rearrange("p (g s) -> p g s", g=A_GROUPS), bb, ALU.add))
                link(dve.tensor_tensor(u, u, v, ALU.mult))
                dve.tensor_tensor(u, u, part("a_z", BW), ALU.mult).then_inc(*dve_s.did("A2"))
                splits(l, j + 5, j + 8)
                j = 8 * CPG
                splits(l, j, j + 4)
                drain(l, 7, col(7), j - 1)
                splits(l, j + 4, j + 5)
                dve.wait_ge(act_s.sem, act_s.at(l, "B1"))
                turned_lo(l, "B1", 6, both(yT[:, 0], 1, 0), both(yT[:, 0], 0, 0), last=False)
                turned_lo(l, "B1", 7, both(yT[:, 0], 1, 2), both(yT[:, 0], 0, 2), last=False)
                turned_lo(l, "B1", 4, both(yT[:, 1], 1, 0), both(yT[:, 1], 0, 0))
                splits(l, j + 5, j + 8)
                j = LATENT0
                n = B_HEADS * QW // 2
                splits(l, j, j + 4)
                drain(l, 8, col(8), j - 1)
                splits(l, j + 4, j + 6)
                drain(l, 9, lat_q[:, 1, 0:n], j + 1)
                splits(l, j + 6, j + 8)
                drain(l, 10, lat_q[:, 1, n:2 * n], j + 3)
                j = LATENT0 + LATENT
                splits(l, j, j + 2)
                drain(l, 11, lat_kv[:, 1, 0:512], j - 3)
                splits(l, j + 2, j + 4)
                drain(l, 12, lat_kv[:, 1, 512:1024], j - 1)
                splits(l, j + 4, j + 5)
                y_turned("yA", 0, 0.125)
                splits(l, j + 5, j + 8)
                times_silu("zB", "b_z")
                j += CPG
                splits(l, j, j + 4)
                drain(l, 13, col(9), j - 1)
                splits(l, j + 4, j + 5)
                dve.wait_ge(pe_s.sem, pe_s.at(l, "B3k"))
                zero_others(krT)
                dve.tensor_copy(knT[:, 2:4].rearrange("p k s -> p (k s)"), bank(7)).then_inc(*dve_s.did("B3k"))
                splits(l, j + 5, j + 8)
                dve.wait_ge(act_drained, l * DRAINS + 13)
                ik = part("c_ik", I_DIM)
                for t in range(TT):
                    last = dve.bn_stats(bn[:, t], ik[:, t])
                link(last)
                own_wait()
                for t in range(TT):
                    last = dve.bn_aggr(mv[:, t], bn[:, t])
                link(last)
                link(dve.tensor_scalar(ms[:, 0:2], mv[:, :, 1], EPS, None, ALU.add))
                link(rsqrt(2))
                for t in range(TT):
                    last = dve.tensor_scalar(ik[:, t], ik[:, t], mv[:, t, 0:1], rs[:, t:t + 1], ALU.subtract, ALU.mult)
                link(last)
                dve.tensor_scalar(iw[:], part("c_iw", I_HEADS), I_HEADS ** -0.5, None, ALU.mult)
                dve.tensor_tensor(ik, ik, g_ik.unsqueeze(1).to_broadcast([P, TT, I_DIM]), ALU.mult).then_inc(*dve_s.did("ikn"))
                j += CPG
                splits(l, j, j + 1)
                dve.wait_ge(pe_s.sem, pe_s.at(l, "B3q"))
                dve.tensor_copy(qnT[:, 2:4].rearrange("p k s -> p (k s)"), bank(6)).then_inc(*dve_s.did("B3q"))
                splits(l, j + 1, j + 4)
                drain(l, 14, col(10), j - 1)
                splits(l, j + 4, j + 5)

                def maxima(name, out_name, b0s, heads, ts, scale):
                    dve.wait_ge(pe_s.sem, pe_s.at(l, name))
                    for t in ts:
                        last = row_max(l, t, heads, 128 * (t + 1), b0s[t])
                    link(last)
                    a, b = ts[0], ts[-1] + 1
                    dve.tensor_scalar(nmx[:, a:b, 0:heads], mx[:, a:b, 0:heads], -scale, None, ALU.mult).then_inc(*dve_s.did(out_name))

                maxima("B4", "B4max", (4, 5), B_HEADS, (0, 1), QW ** -0.5)
                splits(l, j + 5, j + 8)

                def sink_maxima(name, out_name, t):
                    dve.wait_ge(pe_s.sem, pe_s.at(l, name))
                    link(row_max(l, t, D_HEADS, 128 * (t + 1), 4))
                    link(dve.scalar_tensor_tensor(out=mx[:, t], in0=mx[:, t], scalar=D_DIM ** -0.5, in1=sink, op0=ALU.mult, op1=ALU.max))
                    dve.tensor_tensor(ex[:, t], sink, mx[:, t], ALU.subtract)
                    dve.tensor_scalar(nmx[:, t], mx[:, t], -1.0, None, ALU.mult).then_inc(*dve_s.did(out_name))

                def index_score(name, t):
                    width = 128 * (t + 1)
                    dve.wait_ge(act_s.sem, act_s.at(l, name))
                    for h in range(I_HEADS):
                        prev = mask[:, 1, SEQ - width:SEQ] if h == 0 else idx_score[:, t, 0:width]
                        last = dve.scalar_tensor_tensor(out=idx_score[:, t, 0:width], in0=probT[:, h * width:(h + 1) * width],
                                                        scalar=iw[:, t, h:h + 1], in1=prev, op0=ALU.mult, op1=ALU.add)
                        if h < I_HEADS - 1:
                            link(last)
                    last.then_inc(*dve_s.did(name))
                    dve.wait_ge(dve_s.sem, dve_s.at(l, name))

                def select(name, t):
                    width = 128 * (t + 1)
                    src, dst = idx_score[:, t, 0:width], idx_work[:, t, 0:width]
                    for r in range(N_SEL // 8):
                        own_wait()
                        link(dve.max(top[:], src))
                        own_wait()
                        link(dve.match_replace(dst, top[:], src, TAKEN))
                        src = dst
                    link(dve.tensor_scalar(dst, dst, TAKEN, None, ALU.not_equal))
                    dve.tensor_scalar(sel[:, t, 0:width], dst, NEG, None, ALU.mult).then_inc(*dve_s.did(name))

                def merge(G):
                    b, n = G // NG, G % NG
                    dve.wait_ge(act_drained, l * DRAINS + DR_GATE + G + 1)
                    dve.wait_ge(mm_done, l * CHUNKS + GATE0 + (G + 1) * CG + SLOTS)
                    cols = wide[:, :, n * NW:(n + 1) * NW]
                    for t in range(TT):
                        dst = cols[:, t] if b == 0 else gate[:, t]
                        last = dve.scalar_tensor_tensor(out=dst, in0=gate[:, t], scalar=1.0, in1=bank(2 + t), op0=ALU.add, op1=ALU.mult)
                    if b > 0:
                        link(last)
                        last = dve.tensor_tensor(cols, cols, gate[:], ALU.add)
                    last.then_inc(dve_drained, 1)

                for G in range(GATES):
                    j = GATE0 + G * CG
                    splits(l, j, j + 1)
                    if G == 0:
                        dve.wait_ge(act_s.sem, act_s.at(l, "B4"))
                        dve.reciprocal(rinv[:, :, 0:4], sums[:, :, 0:4])
                        dve.wait_ge(pe_s.sem, pe_s.at(l, "B5"))
                        dve.tensor_copy(probT[:, 512:1024], bank(5)).then_inc(*dve_s.did("B5"))
                    splits(l, j + 1, j + 4)
                    if G == 0:
                        drain(l, 15, col(11), j - 1)
                    else:
                        merge(G - 1)
                    splits(l, j + 4, j + 5)
                    if G == 0:
                        dve.wait_ge(dve_s.sem, dve_s.at(l, "B5"))
                        attended("B6", part("b_cq", BW), part("b_z", BW), 4, B_HEADS, (0, 1))
                    if G == 1:
                        dve.wait_ge(pe_s.sem, pe_s.at(l, "C1"))
                        zero_others(cikT)
                        dve.tensor_copy(cqT[:, 2:4].rearrange("p k s -> p (k s)"), bank(5))
                        dve.tensor_copy(ciqT[:, 2:4].rearrange("p k s -> p (k s)"), bank(7)).then_inc(*dve_s.did("C1"))
                    if G == 2:
                        index_score("C3", 0)
                    if G == 3:
                        select("sel1", 1)
                    if G == 4:
                        maxima("C5", "C5max", (4, 5), C_HEADS, (0, 1), C_DIM ** -0.5)
                    if G == 5:
                        attended("C7", part("c_q", BW), part("c_z", BW), 4, C_HEADS, (0, 1))
                    if G == 6:
                        dve.wait_ge(pe_s.sem, pe_s.at(l, "D1"))
                        dve.tensor_copy(dqT[:, 2:4].rearrange("p k s -> p (k s)"), bank(5))
                        by_row = dkT.rearrange("p (j r) s -> p r j s", r=2)
                        zero_others(by_row)
                        for r in range(2):
                            last = dve.tensor_copy(by_row[r * 64:(r + 1) * 64, r],
                                                   ps[r * 64:(r + 1) * 64, 6].rearrange("p (j s) -> p j s", j=D_KV))
                        last.then_inc(*dve_s.did("D1"))
                    if G == 7:
                        dve.wait_ge(act_s.sem, act_s.at(l, "D2"))
                        link(dve.tensor_tensor(sums[:, 0], sums[:, 0], ex[:, 0], ALU.add))
                        dve.reciprocal(rinv[:, 0], sums[:, 0])
                        dve.wait_ge(pe_s.sem, pe_s.at(l, "D4"))
                        dve.tensor_copy(probT[:, 512:1024], bank(5)).then_inc(*dve_s.did("D4"))
                    if G == 8:
                        sink_maxima("D3", "D3max", 1)
                    if G == 9:
                        attended("D6b", part("d_q", BW), part("d_z", BW), 4, D_HEADS, (1,))
                    splits(l, j + 5, j + 8)
                    if G == 0:
                        times_silu("zC", "c_z")
                    if G == 2:
                        select("sel0", 0)
                    splits(l, j + 8, j + 10)
                    if G in (0, 5, 9):
                        y_turned({0: "yB", 5: "yC", 9: "yD"}[G], {0: 1, 5: 0, 9: 1}[G], 0.25)
                    if G == 0:
                        times_silu("zD", "d_z")
                    if G == 2:
                        index_score("C4", 1)
                    if G == 4:
                        dve.wait_ge(act_s.sem, act_s.at(l, "C5"))
                        dve.reciprocal(rinv[:, :, 0:4], sums[:, :, 0:4])
                        dve.wait_ge(pe_s.sem, pe_s.at(l, "C6"))
                        dve.tensor_copy(probT[:, 512:1024], bank(5)).then_inc(*dve_s.did("C6"))
                        dve.wait_ge(dve_s.sem, dve_s.at(l, "C6"))
                    if G == 6:
                        sink_maxima("D2", "D2max", 0)
                    if G == 7:
                        dve.wait_ge(dve_s.sem, dve_s.at(l, "D4"))
                        attended("D6a", part("d_q", BW), part("d_z", BW), 6, D_HEADS, (0,))
                    if G == 8:
                        dve.wait_ge(act_s.sem, act_s.at(l, "D3"))
                        link(dve.tensor_tensor(sums[:, 1], sums[:, 1], ex[:, 1], ALU.add))
                        dve.reciprocal(rinv[:, 1], sums[:, 1])
                        dve.wait_ge(pe_s.sem, pe_s.at(l, "D5"))
                        for b in range(2, 4):
                            last = dve.tensor_copy(probT[:, b * 512:(b + 1) * 512], bank(4 + b))
                        last.then_inc(*dve_s.did("D5"))
                        dve.wait_ge(dve_s.sem, dve_s.at(l, "D5"))
                    if G == GATES - 1:
                        dve.wait_ge(act_s.sem, act_s.at(l, "M0"))
                        for i in range(4):
                            turned_lo(l, "M0", 4 + i, both(lhs, 1, 2 * i), both(lhs, 0, 2 * i), last=(i == 3))
                j = OUT0
                splits(l, j, j + 2)
                merge(GATES - 1)
                dve.wait_ge(act_s.sem, act_s.at(l, "M1"))
                for i in range(2):
                    turned_lo(l, "M1", 4 + i, both(lhs, 1, 8 + 2 * i), both(lhs, 0, 8 + 2 * i), last=(i == 1))
                splits(l, j + 2, j + 4)
                dve.wait_ge(act_s.sem, act_s.at(l, "M2"))
                for i in range(2):
                    turned_lo(l, "M2", 6 + i, both(lhs, 1, 12 + 2 * i), both(lhs, 0, 12 + 2 * i), last=(i == 1))
                splits(l, j + 4, j + 8)

                def out_drain(n):
                    dve.wait_ge(mm_done, l * CHUNKS + OUT0 + (n + 1) * CPG + SLOTS)
                    dve.tensor_copy(wide[:, 1, n * NW:(n + 1) * NW], bank((n % 2) * 2 + 1)).then_inc(dve_drained, 1)

                for n in range(1, NG):
                    j = OUT0 + n * CPG
                    splits(l, j, j + 4)
                    out_drain(n - 1)
                    splits(l, j + 4, j + 8)
                out_drain(NG - 1)
                dve.wait_ge(act_s.sem, act_s.at(l, f"sq{NG - 1}"))
                link(dve.tensor_reduce(ms[:, 0:2], sq[:], AX_X, ALU.add))
                link(dve.tensor_scalar(ms[:, 0:2], ms[:, 0:2], 1.0 / D_MODEL, EPS, ALU.mult, ALU.add))
                link(rsqrt(2))
                dve.wait_ge(pool_s.sem, pool_s.at(l, f"og{NG - 1}"))
                dve.wait_ge(res_loaded, l * 16 + 16)
                for t in range(TT):
                    last = dve.scalar_tensor_tensor(out=wide[:, t], in0=wide[:, t], scalar=rs[:, t:t + 1], in1=area[:, t],
                                                    op0=ALU.mult, op1=ALU.add)
                last.then_inc(*dve_s.did("xn"))
                dve.wait_ge(dve_s.sem, dve_s.at(l, "xn"))
                assert dve_s.n == len(DVE_STEPS)
            assert links[0] == DVE_LINKS, links[0]

        @block.tensor
        def _(pe):
            def chunk(l, j, jn, left, k0, nk, n, b0, first, last):
                s = jn % SLOTS
                pe.wait_ge(lo_done, l * CHUNKS + j + 1 + SLOTS)
                wh = wslot(w_hi, s, nk * n).rearrange("p (k n) -> p k n", k=nk)
                wl = wslot(w_lo, s, nk * n).rearrange("p (k n) -> p k n", k=nk)
                for k in range(nk):
                    for t in range(TT):
                        hi, lo = (left[:, i, k0 + k, t * P:(t + 1) * P] for i in range(2))
                        o = bank(b0 + t, 0, n)
                        a, z = first and k == 0, last and k == nk - 1
                        pe.matmul(o, hi, wh[:, k], start=a, stop=False)
                        pe.matmul(o, hi, wl[:, k], start=False, stop=False)
                        mm = pe.matmul(o, lo, wh[:, k], start=False, stop=z)
                mm.then_inc(mm_done, 1)

            def chunks(l, j0, left, n, b0, a, b, total=CPG):
                for c in range(a, b):
                    chunk(l, j0 + c, j0 + c, left, KC * c, KC, n, b0, c == 0, c == total - 1)

            def pair_free(l, q):
                pe.wait_ge(act_drained, l * DRAINS + q + 1)
                pe.wait_ge(dve_drained, l * DRAINS + q + 1)

            def turn(b, col, src):
                n = src.shape[-1]
                return pe.transpose(ps[0:n, b, col:col + P], src, ident)

            def turn_y(name, src, b0=4):
                for k in range(BKT):
                    for t in range(TT):
                        last = turn(b0 + k // 2, (k % 2) * SEQ + t * P, src[:, t, k * P:(k + 1) * P])
                last.then_inc(*pe_s.did(name))

            def turn_heads(b0, src, n):
                for k in range(n):
                    for t in range(TT):
                        last = turn(b0 + k // 2, (k % 2) * SEQ + t * P, src[:, t, k * P:(k + 1) * P])
                return last

            def seen(step, name):
                pe.wait_ge(step.sem, step.at(l, name))

            def scores(t, heads, b0, m, qk):
                width = 128 * (t + 1)
                per = 512 // width
                for h in range(heads):
                    b = b0 + h // per
                    if h % per == 0:
                        pe.matmul(bank(b), identb, m.unsqueeze(1).to_broadcast([P, per, width]), start=True, stop=True)
                    pairs = qk(h, width)
                    for i, (q, k) in enumerate(pairs):
                        mm = pe.matmul(bank(b, (h % per) * width, width), q, k, start=False,
                                       stop=True, skip_group_check=True)
                return mm

            def turn_prob(t, heads, b0, at):
                width = 128 * (t + 1)
                i = 0
                for h in range(heads):
                    for k in range(t + 1):
                        last = turn(b0 + i // 4, (i % 4) * P, prob[:, at + h * width + k * P:at + h * width + (k + 1) * P])
                        i += 1
                return last

            def weigh(t, heads, b, at, d, value):
                for h in range(heads):
                    for k in range(t + 1):
                        i = h * (t + 1) + k
                        mm = pe.matmul(bank(b, h * d, d), probT[:, at + i * P:at + (i + 1) * P], value(k, h),
                                       start=(k == 0), stop=(k == t))
                return mm

            pe.wait_ge(consts_loaded, 64)
            pe.transpose(ps[:, 0, 0:40], area[0:40, 0, 0:128], tabs[0:40, 0:40]).then_inc(gcols_turned, 1)
            pe.wait_ge(gcols_turned, 2)
            with nc.tensor.Fori(0, DEPTH, 1) as l:
                seen(dve_s, "h0")
                seen(act_s, "h1")
                for b in range(8):
                    for i in range(2):
                        for t in range(TT):
                            k = 2 * b + i
                            last = turn(b, i * SEQ + t * P, area[:, t, k * P:(k + 1) * P])
                    last.then_inc(*pe_s.did(f"hT{b}"))
                seen(act_s, "hT7")
                seen(dve_s, "hT7")
                chunks(l, 0, lhs, MW, 0, 0, CPG)
                with nc.tensor.Fori(0, 2, 1) as i:
                    for h in range(2):
                        if h == 1:
                            pe.wait_ge(act_drained, i * 2 + (l * DRAINS + 1))
                            pe.wait_ge(dve_drained, i * 2 + (l * DRAINS + 1))
                        else:
                            pe.wait_ge(act_drained, i * 2 + (l * DRAINS))
                            pe.wait_ge(dve_drained, i * 2 + (l * DRAINS))
                        for c in range(CPG):
                            chunk(l, i * (2 * CPG) + ((1 + h) * CPG + c), (1 + h) * CPG + c, lhs, KC * c, KC, MW,
                                  2 * ((1 + h) % 2), c == 0, c == CPG - 1)
                for g in range(5, 9):
                    j = g * CPG
                    b0 = 2 * (g % 2)
                    if g == 5:
                        pe.wait_ge(aw_loaded, l * 32 + 32)
                        for i in range(A_GROUPS):
                            last = turn(4, i * P, a_w[:, i // 2, (i % 2) * P:(i % 2 + 1) * P])
                        last.then_inc(*pe_s.did("A1"))
                    if g == 7:
                        seen(dve_s, "vn")
                        for t in range(TT):
                            for i in range(A_GROUPS):
                                mm = pe.matmul(bank(4 + t, i * P, P), a_wT[:, i], part("a_v", BW, t)[:, i * P:(i + 1) * P],
                                               start=True, stop=True)
                        mm.then_inc(*pe_s.did("A2"))
                    if g == 8:
                        seen(dve_s, "Bn")
                        seen(dve_s, "A2")
                        turn_heads(6, part("b_cq", BW), 4)
                        turn_heads(4, part("b_ckv", B_KV_RANK), 2).then_inc(*pe_s.did("B1"))
                    pair_free(l, g - 2)
                    chunks(l, j, lhs, MW, b0, 0, CPG)
                seen(dve_s, "B1")
                j = LATENT0
                for h in range(2):
                    pair_free(l, 7 + h)
                    n = B_HEADS * QW // 2
                    b0 = 2 * ((9 + h) % 2)
                    for c in range(2):
                        chunk(l, j, j, yT[:, 0], KC * c, KC, n, b0, c == 0, c == 1)
                        j += 1
                for h in range(2):
                    pair_free(l, 9 + h)
                    n = B_HEADS * KVW // 2
                    b0 = 2 * ((11 + h) % 2)
                    for c in range(2):
                        chunk(l, j, j, yT[:, 1], c, 1, n, b0, c == 0, c == 1)
                        j += 1
                for g in range(9, MG):
                    j = LATENT0 + LATENT + (g - 9) * CPG
                    q = g + LAT_GROUPS
                    b0 = 2 * (q % 2)
                    if g == 9:
                        turn_y("yA", part("a_u", BW))
                    if g == 10:
                        seen(act_s, "yA")
                        seen(dve_s, "yA")
                        seen(pool_s, "kr")
                        pair_free(l, 12)
                        kv = lat_kv.rearrange("p t (h w) -> p t h w", h=B_HEADS)
                        for h in range(B_HEADS):
                            for t in range(TT):
                                turn(6 + h // 2, (h % 2) * SEQ + t * P, kv[:, t, h, 0:B_NOPE])
                        for t in range(TT):
                            last = turn(4, t * P, kr_twice[:, t])
                        last.then_inc(*pe_s.did("B3k"))
                    if g == 11:
                        seen(act_s, "B3q")
                        seen(dve_s, "B3q")

                        def qk(t):
                            def of_head(h, width):
                                return [(qnT[:, h, t * P:(t + 1) * P], knT[:, h, 0:width]),
                                        (qrT[:, h // 2, t * P:(t + 1) * P], krT[:, h % 2, 0:width])]
                            return of_head
                        scores(0, B_HEADS, 4, mask[:, 1, 128:256], qk(0))
                        scores(1, B_HEADS, 5, mask[:, 1, :], qk(1)).then_inc(*pe_s.did("B4"))
                    pair_free(l, q - 2)
                    chunks(l, j, lhs, MW, b0, 0, 4)
                    if g == 10:
                        seen(act_s, "B3k")
                        seen(dve_s, "B3k")
                        seen(pool_s, "q")
                        qs = lat_q.rearrange("p t (h w) -> p t h w", h=B_HEADS)
                        for h in range(B_HEADS):
                            for t in range(TT):
                                turn(5 + h // 2, (h % 2) * SEQ + t * P, qs[:, t, h, 0:B_NOPE])
                        turn_heads(7, q_rope, 2).then_inc(*pe_s.did("B3q"))
                    if g == 11:
                        seen(act_s, "B4")
                        turn_prob(0, B_HEADS, 4, 0)
                        turn_prob(1, B_HEADS, 5, 512).then_inc(*pe_s.did("B5"))
                    chunks(l, j, lhs, MW, b0, 4, CPG)

                for G in range(GATES):
                    j = GATE0 + G * CG
                    if G == 0:
                        seen(act_s, "B5")
                        seen(dve_s, "B5")
                        kv = lat_kv.rearrange("p t (h w) -> p t h w", h=B_HEADS)
                        weigh(0, B_HEADS, 4, 0, B_V, lambda k, h: kv[:, k, h, B_NOPE:KVW])
                        weigh(1, B_HEADS, 5, 512, B_V, lambda k, h: kv[:, k, h, B_NOPE:KVW]).then_inc(*pe_s.did("B6"))
                    if G == 1:
                        seen(pool_s, "c")
                        seen(act_s, "yB")
                        seen(dve_s, "yB")
                        turn_heads(4, part("c_q", BW), 4)
                        turn_heads(6, part("c_iq", BW), 4).then_inc(*pe_s.did("C1"))
                    if G in (2,):
                        seen(act_s, "C2")

                        def index(t):
                            width = 128 * (t + 1)
                            per = 512 // width
                            for h in range(I_HEADS):
                                mm = pe.matmul(bank(4 + h // per, (h % per) * width, width), ciqT[:, h // 2, t * P:(t + 1) * P],
                                               cikT[:, h % 2, 0:width], start=True, stop=True)
                            return mm
                        index(0).then_inc(*pe_s.did("C3"))
                    if G == 4:
                        seen(dve_s, "sel1")

                        def qk(t):
                            return lambda h, width: [(cqT[:, h, t * P:(t + 1) * P], ckT[:, 0, 0:width])]
                        scores(0, C_HEADS, 4, sel[:, 0, 0:128], qk(0))
                        scores(1, C_HEADS, 5, sel[:, 1, :], qk(1)).then_inc(*pe_s.did("C5"))
                    if G == 5:
                        seen(act_s, "C6")
                        seen(dve_s, "C6")
                        weigh(0, C_HEADS, 4, 0, C_DIM, lambda k, h: part("c_v", C_DIM, k))
                        weigh(1, C_HEADS, 5, 512, C_DIM, lambda k, h: part("c_v", C_DIM, k)).then_inc(*pe_s.did("C7"))
                    if G == 6:
                        seen(pool_s, "d")
                        seen(act_s, "yC")
                        seen(dve_s, "yC")
                        turn_heads(4, part("d_q", BW), 4)
                        turn_heads(6, dk_twice, 2).then_inc(*pe_s.did("D1"))
                    if G == 7:
                        seen(act_s, "D2")
                        turn_prob(0, D_HEADS, 4, 0).then_inc(*pe_s.did("D4"))
                    if G == 8:
                        seen(dve_s, "D6a")

                        def qk(t):
                            def of_head(h, width):
                                return [(dqT[:, h // 2, t * P:(t + 1) * P],
                                         dkT[:, 2 * (h // (D_HEADS // D_KV)) + h % 2, 0:width])]
                            return of_head
                        scores(1, D_HEADS, 4, mask[:, 2, :], qk(1)).then_inc(*pe_s.did("D3"))
                    if G == 9:
                        seen(act_s, "D5")
                        seen(dve_s, "D5")
                        weigh(1, D_HEADS, 4, 0, D_DIM,
                              lambda k, h: part("d_v", 128, k)[:, (h // 4) * 64:(h // 4 + 1) * 64]).then_inc(*pe_s.did("D6b"))
                    if G == 0:
                        pair_free(l, DR_GATE - 2)
                    else:
                        pe.wait_ge(act_drained, l * DRAINS + DR_GATE + G)
                    chunks(l, j, lhs, NW, 0, 0, 5)
                    if G == 0:
                        seen(dve_s, "B6")
                        turn_y("yB", part("b_cq", BW))
                    if G == 1:
                        seen(act_s, "C1")
                        seen(dve_s, "C1")
                        for t in range(TT):
                            turn(4, t * P, part("c_k", C_DIM, t))
                        for t in range(TT):
                            last = turn(4, SEQ + t * P, ik_twice[:, t])
                        last.then_inc(*pe_s.did("C2"))
                    if G == 2:
                        seen(act_s, "C3")
                        index(1).then_inc(*pe_s.did("C4"))
                    if G == 4:
                        seen(act_s, "C5")
                        turn_prob(0, C_HEADS, 4, 0)
                        turn_prob(1, C_HEADS, 5, 512).then_inc(*pe_s.did("C6"))
                    if G == 5:
                        seen(dve_s, "C7")
                        turn_y("yC", part("c_q", BW))
                    if G == 6:
                        seen(act_s, "D1")
                        seen(dve_s, "D1")

                        def qk(t):
                            def of_head(h, width):
                                return [(dqT[:, h // 2, t * P:(t + 1) * P],
                                         dkT[:, 2 * (h // (D_HEADS // D_KV)) + h % 2, 0:width])]
                            return of_head
                        scores(0, D_HEADS, 4, mask[:, 1, 128:256], qk(0)).then_inc(*pe_s.did("D2"))
                    if G == 7:
                        seen(act_s, "D4")
                        seen(dve_s, "D4")
                        weigh(0, D_HEADS, 6, 0, D_DIM,
                              lambda k, h: part("d_v", 128, k)[:, (h // 4) * 64:(h // 4 + 1) * 64]).then_inc(*pe_s.did("D6a"))
                    if G == 8:
                        seen(act_s, "D3")
                        turn_prob(1, D_HEADS, 4, 0).then_inc(*pe_s.did("D5"))
                    if G == 9:
                        seen(dve_s, "D6b")
                        turn_y("yD", part("d_q", BW))
                    chunks(l, j, lhs, NW, 0, 5, CPG)
                    if G == GATES - 1:
                        turn_heads(4, wide, 8).then_inc(*pe_s.did("M0"))
                    b = G // NG
                    if G % NG == 0:
                        seen(dve_s, ("yA", "yB", "yC", "yD")[b])
                    if G == 0:
                        pair_free(l, DR_GATE - 1)
                    else:
                        pe.wait_ge(dve_drained, l * DRAINS + DR_GATE + G)
                    chunks(l, j + CPG, yT[:, b % 2], NW, 2, 0, CPB, CPB)
                seen(dve_s, "M0")
                turn_heads(4, wide[:, :, 2 * NW:3 * NW], 4).then_inc(*pe_s.did("M1"))
                for n in range(NG):
                    if n == 0:
                        pe.wait_ge(act_drained, l * DRAINS + DR_OUT)
                    elif n == 1:
                        pe.wait_ge(dve_drained, l * DRAINS + DR_OUT)
                    else:
                        pair_free(l, DR_OUT + n - 2)
                    j = OUT0 + n * CPG
                    b0 = 2 * (n % 2)
                    if n == 0:
                        chunks(l, j, lhs, NW, b0, 0, 3)
                        pe.wait_ge(dve_drained, l * DRAINS + DR_OUT)
                        turn_heads(6, wide[:, :, 3 * NW:4 * NW], 4).then_inc(*pe_s.did("M2"))
                        chunks(l, j, lhs, NW, b0, 3, 4)
                        seen(dve_s, "M1")
                        chunks(l, j, lhs, NW, b0, 4, 6)
                        seen(dve_s, "M2")
                        chunks(l, j, lhs, NW, b0, 6, CPG)
                    else:
                        chunks(l, j, lhs, NW, b0, 0, CPG)
                assert pe_s.n == len(PE_STEPS)


def constants():
    f = np.float32
    tab = np.zeros((P, 512), f)
    tab[:, 0:128] = np.eye(P, dtype=f)
    pos = np.arange(SEQ, dtype=f)
    for dim, at in ((64, 128), (128, 256)):
        inv = (f(1.0) / (f(10000.0) ** (np.arange(0, dim, 2, dtype=f) / f(dim)))).astype(f)
        ang = (pos[:, None] * inv[None, :]).astype(f)
        for fn, a in ((np.cos, at), (np.sin, at + TT * dim // 2)):
            tab[:, a:a + TT * dim // 2] = fn(ang).astype(f).reshape(TT, P, dim // 2).transpose(1, 0, 2).reshape(P, -1)
    m = np.zeros((P, 3, SEQ), f)
    m[:, 0, 0:P] = np.eye(P, dtype=f)
    chunk = np.arange(SEQ) // CHUNK
    q, k = chunk[P:][:, None], chunk[None, :]
    m[:, 1] = np.where(k <= q, 0.0, NEG)
    m[:, 2] = np.where((k <= q) & (k >= q - 1), 0.0, NEG)
    return tab, m


_INS = ["x", "pre_norm_g", "w_in", "a_ln_g", "a_w_s", "a_b_s", "b_q_norm_g", "b_kv_norm_g", "b_w_uq", "b_w_ukv",
        "c_ik_norm_g", "d_sinks", "w_branch", "w_out", "post_norm_g"]


def kernel(**inputs):
    import concourse.bacc as _bacc
    from concourse.bass_utils import run_bass_kernel_spmd as _run

    nc = _bacc.Bacc("TRN2", target_bir_lowering=False, num_devices=1)
    arrays, args = {}, []
    tab, masks = constants()
    for name, a in [(n, np.ascontiguousarray(inputs[n])) for n in _INS] + [("tables", tab), ("masks", masks)]:
        arrays[f"in_{name}_dram"] = a
        args.append(nc.dram_tensor(f"in_{name}_dram", a.shape, mybir.dt.from_np(a.dtype), kind="ExternalInput").ap())
    args.append(nc.dram_tensor("out_0_dram", (1, SEQ, D_MODEL), F32, kind="ExternalOutput").ap())
    trunk(nc, *args)
    r = _run(nc, [arrays], core_ids=[0])
    return r.results[0]["out_0_dram"]
```

```python
from contextlib import ExitStack

import numpy as np

import concourse.bass as bass
from concourse import mybir

F32 = mybir.dt.float32
F32R = mybir.dt.float32r
BF16 = mybir.dt.bfloat16
I32 = mybir.dt.int32
ALU = mybir.AluOpType
ACT = mybir.ActivationFunctionType
AX_X = mybir.AxisListType.X

P = 128
DEPTH, SEQ, D_MODEL = 2, 256, 2048
TT = SEQ // P
KT = D_MODEL // P
CHUNK = 64
N_BRANCH, BW = 4, 512
BKT = BW // P
A_GROUPS = 4
B_HEADS, B_NOPE, B_ROPE, B_V = 4, 128, 64, 128
B_Q_RANK, B_KV_RANK = 512, 256
QW = B_NOPE + B_ROPE
KVW = B_NOPE + B_V
C_HEADS, C_DIM = 4, 128
I_HEADS, I_DIM = 8, 64
N_SEL = SEQ // 4
D_HEADS, D_KV, D_DIM = 8, 2, 64
EPS = 1e-6
NEG = -1e30
TAKEN = -3e38

COL = {}
_at = 0
for _name, _w in (("a_u", 512), ("a_v", 512), ("a_z", 512), ("b_cq", 512), ("b_ckv", 256), ("b_kr", 64),
                  ("b_z", 512), ("c_q", 512), ("c_k", 128), ("c_v", 128), ("c_iq", 512), ("c_ik", 64),
                  ("c_iw", 8), ("c_z", 512), ("d_q", 512), ("d_k", 128), ("d_v", 128), ("d_z", 512)):
    COL[_name] = _at
    _at += _w
MIX = _at

KC = 2
NW = 512
MG = 12
MW = MIX // MG
SLOTS = 4
CPG = KT // KC
NG = D_MODEL // NW
GATES = N_BRANCH * NG
LATENT_AT = 9
LATENT = 8
CPB = BKT // KC
CG = CPG + CPB
LATENT0 = LATENT_AT * CPG
GATE0 = MG * CPG + LATENT
OUT0 = GATE0 + GATES * CG
CHUNKS = OUT0 + NG * CPG
assert MW * MG == MIX and CHUNKS % SLOTS == 0 and LATENT0 % SLOTS == 0 and MW % 2 == 0

LAT_GROUPS = 4
DR_GATE = MG + LAT_GROUPS
DR_OUT = DR_GATE + GATES
DRAINS = DR_OUT + NG
PAIRS = 2

GELU_C, GELU_S = 0.044715, float(np.sqrt(2.0 / np.pi))

PE_STEPS = ([f"hT{b}" for b in range(8)] +
            ["A1", "A2", "B1", "yA", "B3k", "B3q", "B4", "B5", "B6", "yB",
             "C1", "C2", "C3", "C4", "C5", "C6", "C7", "yC",
             "D1", "D2", "D4", "D6a", "D3", "D5", "D6b", "yD", "M0", "M1", "M2", "out3"])
ACT_STEPS = (["gains"] + [f"hT{b}" for b in range(8)] +
             ["ss", "gelu", "zA", "B1", "zB", "yA", "B3k", "B3q", "B4", "zC", "B5", "zD", "yB",
              "C1", "C2", "C3", "C4", "C5", "C6", "yC", "D1", "D2", "D4", "D3", "D5", "yD",
              "M0", "M1", "M2"] + [f"sq{n}{t}" for n in range(4) for t in range(2)])
DVE_STEPS = (["hT0", "hT1", "xn1", "hT2", "hT3", "xn2", "hT4", "hT5", "xn3", "hT6", "hT7", "rn",
              "A1", "gelu", "vn", "zA", "Bn", "A2", "B1", "yA", "zB", "B3k", "ikn", "B3q", "B4max",
              "B5", "B6", "zC", "yB", "zD", "C1", "C3", "sel0", "C4", "sel1", "C5max", "C6", "C7", "yC",
              "D1", "D2max", "D4", "D6a", "D3max", "D5", "D6b", "yD", "M0", "M1", "M2"] +
             [f"og{n}" for n in range(3)])
POOL_STEPS = ["mask", "gelu", "kr", "q", "c", "d"]


class Steps:

    def __init__(self, sem, names):
        self.sem, self.names, self.n = sem, names, 0

    def did(self, name):
        assert self.names[self.n] == name, (self.names[self.n], name)
        self.n += 1
        return self.sem, 1

    def at(self, layer, name):
        return layer * len(self.names) + (self.names.index(name) + 1)


def trunk(nc, x, pre_norm_g, w_in, a_ln_g, a_w_s, a_b_s, b_q_norm_g, b_kv_norm_g, b_w_uq, b_w_ukv,
          c_ik_norm_g, d_sinks, w_branch, w_out, post_norm_g, tables, masks, out):
    with ExitStack() as ctx:
        def sb(name, shape, dt=F32):
            return ctx.enter_context(nc.sbuf_tensor(name, shape, dt))

        def sem(name):
            return ctx.enter_context(nc.semaphore(name))

        wide = sb("wide", [P, TT, D_MODEL])
        area = sb("area", [P, TT, D_MODEL])
        lhs = sb("lhs", [P, 2, KT, SEQ], F32R)
        yT = sb("yT", [P, 2, 2, BKT, SEQ], F32R)
        raw = sb("raw", [P, SLOTS, KC * NW])
        w_hi = sb("w_hi", [P, SLOTS, KC * NW], F32R)
        w_lo = sb("w_lo", [P, SLOTS, KC * NW], F32R)
        proj = sb("proj", [P, TT, MIX])
        gate = sb("gate", [P, TT, NW])
        turned = sb("turned", [P, 12 * SEQ])
        tmp = sb("tmp", [P, 2, NW])
        gains = sb("gains", [P, 1352])
        tabs = sb("tabs", [P, 512])
        mask = sb("mask", [P, 3, SEQ], BF16)
        sel = sb("sel", [P, TT, SEQ], BF16)
        gcols = sb("gcols", [P, 40])
        gcol = sb("gcol", [P, KT])
        bcol = sb("bcol", [P, A_GROUPS])
        ms = sb("ms", [P, 4])
        rn = sb("rn", [P, TT])
        rn_half = sb("rn_half", [P, TT])
        rs = sb("rs", [P, 4])
        half = sb("half", [P, 4], I32)
        nt = sb("nt", [P, 4])
        mh = sb("mh", [P, 4])
        ss = sb("ss", [P, TT, 2])
        sq = sb("sq", [P, TT, NG])
        bn = sb("bn", [P, TT, 6])
        mv = sb("mv", [P, TT, 2])
        mx = sb("mx", [P, TT, 8])
        nmx = sb("nmx", [P, TT, 8])
        ex = sb("ex", [P, TT, 8])
        sums = sb("sums", [P, TT, 8])
        rinv = sb("rinv", [P, TT, 8])
        iw = sb("iw", [P, TT, I_HEADS])
        top = sb("top", [P, 8])
        ps = ctx.enter_context(nc.psum_tensor("ps", [P, 8, 512], F32))

        consts_loaded, x_stored, out_stored = sem("consts_loaded"), sem("x_stored"), sem("out_stored")
        head_ready = sem("head_ready")
        masks_loaded = sem("masks_loaded")
        wide_cleared, out_ready = sem("wide_cleared"), sem("out_ready")
        raw_loaded = [sem(f"raw_loaded{s}") for s in range(SLOTS)]
        hi_done, lo_done, mm_done = sem("hi_done"), sem("lo_done"), sem("mm_done")
        act_drained, dve_drained = sem("act_drained"), sem("dve_drained")
        aw_loaded, gains_loaded, post_loaded = sem("aw_loaded"), sem("gains_loaded"), sem("post_loaded")
        res_loaded = [sem(f"res_loaded{n}") for n in range(NG)]
        gcols_turned = sem("gcols_turned")
        dve_link, pool_link = sem("dve_link"), sem("pool_link")
        dve_waited, pool_waited = sem("dve_waited"), sem("pool_waited")
        pe_s, act_s = Steps(sem("pe_steps"), PE_STEPS), Steps(sem("act_steps"), ACT_STEPS)
        dve_s, pool_s = Steps(sem("dve_steps"), DVE_STEPS), Steps(sem("pool_steps"), POOL_STEPS)

        ident = tabs[:, 0:128]
        identb = mask[:, 0, 0:128]
        cos64 = tabs[:, 128:192].rearrange("p (t d) -> p t d", t=TT)
        sin64 = tabs[:, 192:256].rearrange("p (t d) -> p t d", t=TT)
        cos128 = tabs[:, 256:384].rearrange("p (t d) -> p t d", t=TT)
        sin128 = tabs[:, 384:512].rearrange("p (t d) -> p t d", t=TT)
        g_ln, g_q, g_kv, g_ik, sink = (gains[:, 0:512], gains[:, 512:1024], gains[:, 1024:1280],
                                       gains[:, 1280:1344], gains[:, 1344:1352])

        def part(name, w, t=slice(None)):
            return proj[:, t, COL[name]:COL[name] + w]

        gelu_arg = wide[:, :, 0:2 * BW]
        lat_q = wide[:, :, 0:B_HEADS * QW]
        lat_kv = wide[:, :, 768:768 + B_HEADS * KVW]
        a_w = wide[:, :, 1792:2048]
        q_rope = wide[:, :, 1792:2048]
        idx_score, idx_work = proj[:, :, 512:768], proj[:, :, 1024:1280]
        ik_twice, kr_twice = proj[:, :, 1280:1408], proj[:, :, 1408:1536]
        dk_twice = proj[:, :, COL["b_ckv"]:COL["b_ckv"] + 256]
        prob, probT = area[:, 0], area[:, 1]
        post_g = proj[:, 0, 0:D_MODEL]

        gain_rows = proj[0:40, 0, 0:P]
        mask_rows = proj[:, 1, 0:3 * SEQ].rearrange("p (i s) -> p i s", i=3)

        def rows(at, n):
            return turned[:, at * SEQ:(at + n) * SEQ].rearrange("p (k s) -> p k s", k=n)

        a_wT = rows(0, 2).rearrange("p k (h s) -> p (k h) s", h=2)
        qnT, qrT, knT, krT = rows(0, 4), rows(4, 2), rows(6, 4), rows(10, 2)
        cqT, ckT, cikT, ciqT = rows(0, 4), rows(4, 1), rows(5, 2), rows(7, 4)
        dqT, dkT = rows(0, 4), rows(4, 4)

        def bank(b, a=0, n=512):
            return ps[:, b, a:a + n]

        def wslot(buf, slot, n):
            return buf[:, slot, 0:n]

        def w_width(j):
            if LATENT0 <= j < LATENT0 + LATENT // 2:
                return KC * (B_HEADS * QW // 2)
            if LATENT0 + LATENT // 2 <= j < LATENT0 + LATENT:
                return B_HEADS * KVW // 2
            if j < GATE0:
                return KC * MW
            return KC * NW

        def load_residual(eng, src, n):
            c = slice(n * NW, (n + 1) * NW)
            eng.dma_start(area[:, :, c], src[0].rearrange("(t p) d -> p t d", p=P)[:, :, c]).then_inc(res_loaded[n], 16)

        block = ctx.enter_context(nc.Block())

        @block.sync
        def _(sp):
            load_residual(sp, x, 0)
            sp.dma_start(tabs[:], tables).then_inc(consts_loaded, 16)
            sp.dma_start(gain_rows[0:DEPTH * KT], pre_norm_g.rearrange("l (k p) -> (l k) p", p=P)).then_inc(consts_loaded, 16)
            sp.dma_start(gain_rows[DEPTH * KT:40], a_b_s.rearrange("l g p -> (l g) p")).then_inc(consts_loaded, 16)

            def load(l, j, slot, src, n):
                sp.wait_ge(lo_done, l * CHUNKS + j + 1)
                dst = wslot(raw, slot, n)
                k = src.shape[1]
                sp.dma_start(dst.rearrange("p (k n) -> p k n", k=k), src).then_inc(raw_loaded[slot], 16)

            def of(w, l, k0, nk, c0, n):
                return w[bass.ds(l, 1), k0 * P:(k0 + nk) * P, bass.ds(c0, n)].rearrange("a (k p) n -> p (a k) n", p=P)

            with nc.sync.Fori(0, DEPTH, 1) as l:
                def mix_groups(g0, n, j0):
                    with nc.sync.Fori(0, n, 1) as g:
                        for c in range(CPG):
                            load(l, j0 + c + g * CPG, c % SLOTS, of(w_in, l, KC * c, KC, g0 * MW + g * MW, MW), KC * MW)
                mix_groups(0, LATENT_AT, 0)
                j = LATENT0
                for h in range(2):
                    for c in range(2):
                        n = B_HEADS * QW // 2
                        src = b_w_uq[bass.ds(l, 1), KC * c * P:KC * (c + 1) * P].rearrange(
                            "a (k p) h d -> p (a k) (h d)", p=P)[:, :, h * n:(h + 1) * n]
                        load(l, j, j % SLOTS, src, KC * n)
                        j += 1
                for h in range(2):
                    for c in range(2):
                        n = B_HEADS * KVW // 2
                        src = b_w_ukv[bass.ds(l, 1), c * P:(c + 1) * P].rearrange(
                            "a p h d -> p a (h d)")[:, :, h * n:(h + 1) * n]
                        load(l, j, j % SLOTS, src, n)
                        j += 1
                mix_groups(LATENT_AT, MG - LATENT_AT, LATENT0 + LATENT)
                with nc.sync.Fori(0, GATES // 2, 1) as g2:
                    for h in range(2):
                        for c in range(CG):
                            j = GATE0 + h * CG + c + g2 * (2 * CG)
                            if c < CPG:
                                src = of(w_in, l, KC * c, KC, g2 * (2 * NW) + (MIX + h * NW), NW)
                            else:
                                k0 = KC * (c - CPG)
                                src = w_branch[bass.ds(l, 1), bass.ds(g2 // 2, 1), k0 * P:(k0 + KC) * P,
                                               bass.ds((g2 % 2) * (2 * NW) + h * NW, NW)].rearrange(
                                    "a b (k p) n -> p (a b k) n", p=P)
                            load(l, j, (GATE0 + h * CG + c) % SLOTS, src, KC * NW)
                sp.wait_ge(dve_s.sem, dve_s.at(l, "yD"))
                sp.wait_ge(x_stored, l * (NG * 16) + NG * 16)
                for n in range(NG):
                    load_residual(sp, out, n)
                with nc.sync.Fori(0, NG, 1) as g:
                    for c in range(CPG):
                        load(l, OUT0 + c + g * CPG, c % SLOTS, of(w_out, l, KC * c, KC, g * NW, NW), KC * NW)
            for i in range(2):
                c = slice(i * NW // 2, (i + 1) * NW // 2)
                sp.wait_ge(head_ready, 2 * DEPTH + i + 1)
                sp.dma_start(out[0].rearrange("(t p) d -> p t d", p=P)[:, :, c], wide[:, :, c]).then_inc(out_stored, 16)
            for n in range(1, NG):
                for t in range(TT):
                    c = slice(n * NW, (n + 1) * NW)
                    sp.wait_ge(out_ready, (n - 1) * TT + t + 1)
                    sp.dma_start(out[0, t * P:(t + 1) * P, c], wide[:, t, c]).then_inc(out_stored, 16)
            sp.wait_ge(out_stored, (2 + (NG - 1) * TT) * 16)

        @block.gpsimd
        def _(pool):
            links = [0]
            POOL_LINKS = 30

            def link(ins):
                links[0] += 1
                ins.then_inc(pool_link, 1)
                pool.wait_ge(pool_link, l * POOL_LINKS + links[0])

            def rope(dst, src, cos, sin, t, heads, d, copies=1, step=None):
                def halves(ap):
                    return ap.rearrange("p (h e d) -> p h e d", h=heads, e=2)
                hd = d // 2
                a = tmp[:, 0, 0:heads * d].rearrange("p (h e d) -> p h e d", h=heads, e=2)
                b = tmp[:, 1, 0:heads * d].rearrange("p (h e d) -> p h e d", h=heads, e=2)
                c4 = cos[:, t].unsqueeze(1).unsqueeze(1).to_broadcast([P, heads, 2, hd])
                s3 = sin[:, t].unsqueeze(1).to_broadcast([P, heads, hd])
                pool.tensor_tensor(a, src, c4, ALU.mult)
                pool.tensor_tensor(b[:, :, 0], src[:, :, 1], s3, ALU.mult)
                link(pool.tensor_tensor(b[:, :, 1], src[:, :, 0], s3, ALU.mult))
                for i in range(copies):
                    pool.tensor_tensor(dst[i][:, :, 0], a[:, :, 0], b[:, :, 0], ALU.subtract)
                    last = pool.tensor_tensor(dst[i][:, :, 1], a[:, :, 1], b[:, :, 1], ALU.add)
                return last

            def split_heads(ap, heads):
                return ap.rearrange("p (h e d) -> p h e d", h=heads, e=2)

            pool.memset(tmp[:, 0, 0:8], 0.0).then_inc(lo_done, SLOTS)
            pool.memset(tmp[:, 0, 8:16], 0.0).then_inc(act_drained, PAIRS)
            pool.memset(tmp[:, 0, 16:24], 0.0).then_inc(dve_drained, PAIRS)
            pool.memset(wide[:, 0], 0.0).then_inc(wide_cleared, 1)
            with nc.gpsimd.Fori(0, DEPTH, 1) as l:
                pool.wait_ge(hi_done, l * CHUNKS + 1)
                n = w_width(0)
                pool.tensor_tensor(wslot(w_lo, 0, n), wslot(raw, 0, n), wslot(w_hi, 0, n).bitcast(F32),
                                   ALU.subtract).then_inc(lo_done, 1)
                def store(n):
                    c = slice(n * NW, (n + 1) * NW)
                    if n == 0:
                        pool.wait_ge(head_ready, l * 2 + 2)
                    else:
                        pool.wait_ge(dve_s.sem, dve_s.at(l, f"xn{n}"))
                    pool.sem_inc(pool_waited, 1)
                    pool.dma_start(out[0].rearrange("(t p) d -> p t d", p=P)[:, :, c], wide[:, :, c]).then_inc(x_stored, 16)

                store(0)
                pool.dma_start(mask_rows, masks).then_inc(masks_loaded, 16)
                store(1)
                pool.wait_ge(masks_loaded, l * 16 + 16)
                pool.sem_inc(pool_waited, 1)
                pool.tensor_copy(mask[:], mask_rows).then_inc(*pool_s.did("mask"))
                store(2)
                store(3)
                pool.wait_ge(pe_s.sem, pe_s.at(l, "hT7"))
                pool.wait_ge(act_s.sem, act_s.at(l, "ss"))
                pool.wait_ge(x_stored, l * (NG * 16) + NG * 16)
                for t in range(TT):
                    pool.dma_start(a_w[:, t].rearrange("p (g s) -> p g s", g=2),
                                   a_w_s[bass.ds(l, 1), 2 * t:2 * t + 2].rearrange("a g t s -> t (a g) s")).then_inc(aw_loaded, 16)
                for dst, src in ((g_ln, a_ln_g), (g_q, b_q_norm_g), (g_kv, b_kv_norm_g), (g_ik, c_ik_norm_g), (sink, d_sinks)):
                    pool.dma_start(dst, src[bass.ds(l, 1)].to_broadcast([P, src.shape[1]])).then_inc(gains_loaded, 16)
                pool.wait_ge(act_drained, l * DR_OUT + 4 + PAIRS)
                pool.wait_ge(dve_drained, l * DRAINS + 4 + PAIRS)
                uv = proj[:, :, 0:2 * BW]
                link(pool.tensor_tensor(gelu_arg, uv, uv, ALU.mult))
                pool.sem_inc(pool_waited, 1)
                link(pool.tensor_scalar(gelu_arg, gelu_arg, GELU_C, 1.0, ALU.mult, ALU.add))
                pool.tensor_tensor(gelu_arg, gelu_arg, uv, ALU.mult).then_inc(*pool_s.did("gelu"))
                pool.wait_ge(dve_s.sem, dve_s.at(l, "A2"))
                for t in range(TT):
                    kr = split_heads(part("b_kr", B_ROPE, t), 1)
                    last = rope([split_heads(kr_twice[:, t, i * 64:(i + 1) * 64], 1) for i in range(2)],
                                kr, cos64, sin64, t, 1, B_ROPE, copies=2)
                    if t + 1 < TT:
                        link(last)
                last.then_inc(*pool_s.did("kr"))
                pool.wait_ge(pool_s.sem, pool_s.at(l, "kr"))
                pool.wait_ge(act_drained, l * DR_OUT + LATENT_AT + 2 + PAIRS)
                pool.wait_ge(dve_drained, l * DRAINS + LATENT_AT + 2 + PAIRS)
                for t in range(TT):
                    src = lat_q[:, t].rearrange("p (h w) -> p h w", h=B_HEADS)[:, :, B_NOPE:QW].rearrange(
                        "p h (e d) -> p h e d", e=2)
                    last = rope([split_heads(q_rope[:, t], B_HEADS)], src, cos64, sin64, t, B_HEADS, B_ROPE)
                    if t + 1 < TT:
                        link(last)
                last.then_inc(*pool_s.did("q"))
                pool.wait_ge(pool_s.sem, pool_s.at(l, "q"))
                pool.wait_ge(act_drained, l * DR_OUT + 14 + PAIRS)
                pool.wait_ge(dve_drained, l * DRAINS + 14 + PAIRS)
                pool.wait_ge(dve_s.sem, dve_s.at(l, "ikn"))
                for t in range(TT):
                    for name, heads, d, co, si in (("c_q", C_HEADS, C_DIM, cos128, sin128), ("c_k", 1, C_DIM, cos128, sin128),
                                                   ("c_iq", I_HEADS, I_DIM, cos64, sin64)):
                        v = split_heads(part(name, heads * d, t), heads)
                        link(rope([v], v, co, si, t, heads, d))
                    v = split_heads(part("c_ik", I_DIM, t), 1)
                    last = rope([split_heads(ik_twice[:, t, i * 64:(i + 1) * 64], 1) for i in range(2)],
                                v, cos64, sin64, t, 1, I_DIM, copies=2)
                    if t + 1 < TT:
                        link(last)
                last.then_inc(*pool_s.did("c"))
                pool.wait_ge(pool_s.sem, pool_s.at(l, "c"))
                pool.wait_ge(act_drained, l * DR_OUT + DR_GATE + PAIRS)
                pool.wait_ge(dve_drained, l * DRAINS + DR_GATE + PAIRS)
                for t in range(TT):
                    v = split_heads(part("d_q", D_HEADS * D_DIM, t), D_HEADS)
                    link(rope([v], v, cos64, sin64, t, D_HEADS, D_DIM))
                    v = split_heads(part("d_k", D_KV * D_DIM, t), D_KV)
                    twice = dk_twice[:, t].rearrange("p (h i e d) -> p i h e d", h=D_KV, i=2, e=2)
                    last = rope([twice[:, 0], twice[:, 1]], v, cos64, sin64, t, D_KV, D_DIM, copies=2)
                    if t + 1 < TT:
                        link(last)
                last.then_inc(*pool_s.did("d"))
                pool.wait_ge(dve_s.sem, dve_s.at(l, "yD"))
                pool.dma_start(post_g, post_norm_g[bass.ds(l, 1)].to_broadcast([P, D_MODEL])).then_inc(post_loaded, 16)
            assert links[0] == POOL_LINKS, links[0]

        @block.scalar
        def _(act):

            def split(l, j, jn=None):
                jn = j if jn is None else jn
                n, s = w_width(jn), jn % SLOTS
                act.wait_ge(raw_loaded[s], (l * CHUNKS + (j - s)) * (16 // SLOTS) + 16)
                act.wait_ge(mm_done, l * CHUNKS + j + 1)
                act.activation(wslot(w_hi, s, n), wslot(raw, s, n), ACT.Copy).then_inc(hi_done, 1)

            def splits(l, a, b):
                for j in range(a, b):
                    split(l, j)

            def drain(l, q, dst, seen, scale=1.0):
                act.wait_ge(mm_done, l * CHUNKS + seen + 1 + SLOTS)
                act.activation(dst, bank((q % 2) * 2, 0, dst.shape[-1]), ACT.Copy, scale=scale).then_inc(act_drained, 1)

            def turned_hi(l, name, b, dst, scale=1.0, last=True):
                act.wait_ge(pe_s.sem, pe_s.at(l, name))
                ins = act.activation(dst, bank(b), ACT.Copy, scale=scale)
                if last:
                    ins.then_inc(*act_s.did(name))

            def softmax(t, heads, b0, at, scale):
                width = P * (t + 1)
                per = 512 // width
                for h in range(heads):
                    last = act.activation(prob[:, at + h * width:at + (h + 1) * width],
                                          bank(b0 + h // per, (h % per) * width, width), ACT.Exp,
                                          bias=nmx[:, t, h:h + 1], scale=scale, accum_out=sums[:, t, h:h + 1])
                return last

            def half_tanh(name, part_name):
                act.activation(gate[:], part(part_name, BW), ACT.Tanh, scale=0.5).then_inc(*act_s.did(name))

            def evac(dst, b, a=0, n=512):
                return act.activation(dst, bank(b, a, n), ACT.Copy)

            act.wait_ge(res_loaded[0], 16)
            for n in range(1, NG):
                load_residual(act, x, n)
            with nc.scalar.Fori(0, DEPTH, 1) as l:
                def input_hi(b):
                    act.wait_ge(pe_s.sem, pe_s.at(l, f"hT{b}"))
                    for i in range(2):
                        k = 2 * b + i
                        last = act.activation(lhs[:, 0, k], bank(4 + b % 4, i * SEQ, SEQ), ACT.Copy, scale=gcol[:, k:k + 1])
                    last.then_inc(*act_s.did(f"hT{b}"))

                act.wait_ge(gcols_turned, 2)
                act.activation(gcol[:], gcols[:, bass.ds(l * KT, KT)], ACT.Copy)
                act.activation(bcol[:], gcols[:, bass.ds(l * A_GROUPS + DEPTH * KT, A_GROUPS)], ACT.Copy).then_inc(*act_s.did("gains"))
                splits(l, 0, 1)
                act.wait_ge(act_s.sem, act_s.at(l, "gains"))
                input_hi(0)
                input_hi(1)
                splits(l, 1, 3)
                input_hi(2)
                input_hi(3)
                splits(l, 3, 5)
                input_hi(4)
                input_hi(5)
                splits(l, 5, 7)

                def squares(part, c, step):
                    act.wait_ge(dve_s.sem, dve_s.at(l, step))
                    for t in range(TT):
                        last = act.activation(area[:, t, c], wide[:, t, c], ACT.Square, accum_out=ss[:, t, part:part + 1])
                    return last
                squares(0, slice(0, 3 * NW), "xn2")
                input_hi(6)
                input_hi(7)
                splits(l, 7, 8)
                squares(1, slice(3 * NW, D_MODEL), "xn3").then_inc(*act_s.did("ss"))
                with nc.scalar.Fori(0, 2, 1) as i:
                    for h in range(2):
                        j0 = (1 + h) * CPG
                        for c in range(4):
                            split(l, i * (2 * CPG) + (j0 + c), j0 + c)
                        act.wait_ge(dve_s.sem, dve_s.at(l, "rn"))
                        act.wait_ge(mm_done, (l * CHUNKS + (j0 + SLOTS)) + i * (2 * CPG))
                        act.activation(proj[:, 0, bass.ds(i * (2 * MW) + h * MW, MW)], bank(h * 2, 0, MW), ACT.Copy,
                                       scale=rn[:, 0:1]).then_inc(act_drained, 1)
                        for c in range(4, CPG):
                            split(l, i * (2 * CPG) + (j0 + c), j0 + c)

                rn_of_tile = rn[:, 0:1]

                def col(g):
                    return proj[:, 0, g * MW:(g + 1) * MW]
                j = 5 * CPG
                splits(l, j, j + 4)
                drain(l, 4, col(4), j - 1, rn_of_tile)
                splits(l, j + 4, j + 5)
                act.wait_ge(pool_s.sem, pool_s.at(l, "gelu"))
                act.activation(gelu_arg, gelu_arg, ACT.Tanh, scale=GELU_S).then_inc(*act_s.did("gelu"))
                splits(l, j + 5, j + 8)
                half_tanh("zA", "a_z")
                for g in (6, 7, 8):
                    j = g * CPG
                    splits(l, j, j + 4)
                    drain(l, g - 1, col(g - 1), j - 1, rn_of_tile)
                    splits(l, j + 4, j + 5)
                    if g == 8:
                        turned_hi(l, "B1", 6, yT[:, 0, 0, 0:2].rearrange("p k s -> p (k s)"), last=False)
                        turned_hi(l, "B1", 7, yT[:, 0, 0, 2:4].rearrange("p k s -> p (k s)"), last=False)
                        turned_hi(l, "B1", 4, yT[:, 1, 0, 0:2].rearrange("p k s -> p (k s)"))
                    splits(l, j + 5, j + 8)
                act.wait_ge(dve_s.sem, dve_s.at(l, "Bn"))
                half_tanh("zB", "b_z")
                j = LATENT0
                n = B_HEADS * QW // 2
                splits(l, j, j + 4)
                drain(l, 8, col(8), j - 1, rn_of_tile)
                splits(l, j + 4, j + 6)
                drain(l, 9, lat_q[:, 0, 0:n], j + 1)
                splits(l, j + 6, j + 8)
                drain(l, 10, lat_q[:, 0, n:2 * n], j + 3)
                j = LATENT0 + LATENT
                splits(l, j, j + 2)
                drain(l, 11, lat_kv[:, 0, 0:512], j - 3)
                splits(l, j + 2, j + 4)
                drain(l, 12, lat_kv[:, 0, 512:1024], j - 1)
                splits(l, j + 4, j + 5)
                for i in range(2):
                    turned_hi(l, "yA", 4 + i, yT[:, 0, 0, 2 * i:2 * i + 2].rearrange("p k s -> p (k s)"), 0.125, last=(i == 1))
                splits(l, j + 5, j + 8)
                j += CPG
                splits(l, j, j + 4)
                drain(l, 13, col(9), j - 1, rn_of_tile)
                splits(l, j + 4, j + 5)
                act.wait_ge(pe_s.sem, pe_s.at(l, "B3k"))
                evac(knT[:, 0:2].rearrange("p k s -> p (k s)"), 6)
                for r in range(2):
                    last = act.activation(krT[r * 64:(r + 1) * 64, r], ps[r * 64:(r + 1) * 64, 4, 0:SEQ], ACT.Copy)
                last.then_inc(*act_s.did("B3k"))
                splits(l, j + 5, j + 8)
                j += CPG
                splits(l, j, j + 1)
                act.wait_ge(pe_s.sem, pe_s.at(l, "B3q"))
                evac(qnT[:, 0:2].rearrange("p k s -> p (k s)"), 5)
                evac(qrT[:].rearrange("p k s -> p (k s)"), 7).then_inc(*act_s.did("B3q"))
                splits(l, j + 1, j + 4)
                drain(l, 14, col(10), j - 1, rn_of_tile)
                splits(l, j + 4, j + 5)
                act.wait_ge(dve_s.sem, dve_s.at(l, "B4max"))
                softmax(0, B_HEADS, 4, 0, QW ** -0.5)
                softmax(1, B_HEADS, 5, 512, QW ** -0.5).then_inc(*act_s.did("B4"))
                splits(l, j + 5, j + 8)
                act.wait_ge(dve_s.sem, dve_s.at(l, "zB"))
                half_tanh("zC", "c_z")

                for G in range(GATES):
                    j = GATE0 + G * CG
                    splits(l, j, j + 1)
                    if G == 0:
                        act.wait_ge(pe_s.sem, pe_s.at(l, "B5"))
                        evac(probT[:, 0:512], 4)
                        evac(probT[:, 1024:1536], 6).then_inc(*act_s.did("B5"))
                    splits(l, j + 1, j + 2)
                    if G > 0:
                        act.wait_ge(mm_done, l * CHUNKS + (j - 3) + 1 + SLOTS)
                        if G == 1:
                            act.wait_ge(dve_s.sem, dve_s.at(l, "zD"))
                        else:
                            act.wait_ge(dve_drained, l * DRAINS + DR_GATE + G - 1 + PAIRS)
                        for t in range(TT):
                            last = act.activation(gate[:, t], bank(t), ACT.Tanh, scale=rn_half[:, t:t + 1])
                        last.then_inc(act_drained, 1)
                    splits(l, j + 2, j + 4)
                    if G == 0:
                        drain(l, 15, col(11), j - 1, rn_of_tile)
                    splits(l, j + 4, j + 5)
                    if G == 1:
                        act.wait_ge(pe_s.sem, pe_s.at(l, "C1"))
                        evac(cqT[:, 0:2].rearrange("p k s -> p (k s)"), 4)
                        evac(ciqT[:, 0:2].rearrange("p k s -> p (k s)"), 6).then_inc(*act_s.did("C1"))
                    if G == 2:
                        act.wait_ge(pe_s.sem, pe_s.at(l, "C3"))
                        act.activation(probT[:, 0:512], bank(4), ACT.Relu, scale=I_DIM ** -0.5)
                        act.activation(probT[:, 512:1024], bank(5), ACT.Relu, scale=I_DIM ** -0.5).then_inc(*act_s.did("C3"))
                    if G == 4:
                        act.wait_ge(dve_s.sem, dve_s.at(l, "C5max"))
                        softmax(0, C_HEADS, 4, 0, C_DIM ** -0.5)
                        softmax(1, C_HEADS, 5, 512, C_DIM ** -0.5).then_inc(*act_s.did("C5"))
                    if G == 6:
                        act.wait_ge(pe_s.sem, pe_s.at(l, "D1"))
                        evac(dqT[:, 0:2].rearrange("p k s -> p (k s)"), 4).then_inc(*act_s.did("D1"))
                    if G == 7:
                        act.wait_ge(pe_s.sem, pe_s.at(l, "D4"))
                        evac(probT[:, 0:512], 4).then_inc(*act_s.did("D4"))
                    if G == 8:
                        act.wait_ge(dve_s.sem, dve_s.at(l, "D3max"))
                        act.activation(ex[:, 1], ex[:, 1], ACT.Exp)
                        softmax(1, D_HEADS, 4, 0, D_DIM ** -0.5).then_inc(*act_s.did("D3"))
                    splits(l, j + 5, j + 8)
                    if G == 0:
                        act.wait_ge(dve_s.sem, dve_s.at(l, "zC"))
                        half_tanh("zD", "d_z")
                    splits(l, j + 8, j + 10)
                    if G in (0, 5, 9):
                        name, buf, b0 = {0: ("yB", 1, 4), 5: ("yC", 0, 4), 9: ("yD", 1, 4)}[G]
                        for i in range(2):
                            turned_hi(l, name, b0 + i, yT[:, buf, 0, 2 * i:2 * i + 2].rearrange("p k s -> p (k s)"), 0.25, last=(i == 1))
                    if G == 1:
                        act.wait_ge(pe_s.sem, pe_s.at(l, "C2"))
                        evac(ckT[:, 0], 4, 0, SEQ)
                        for r in range(2):
                            last = act.activation(cikT[r * 64:(r + 1) * 64, r], ps[r * 64:(r + 1) * 64, 4, SEQ:2 * SEQ], ACT.Copy)
                        last.then_inc(*act_s.did("C2"))
                    if G == 2:
                        act.wait_ge(pe_s.sem, pe_s.at(l, "C4"))
                        act.wait_ge(dve_s.sem, dve_s.at(l, "C3"))
                        for b in range(4):
                            last = act.activation(probT[:, b * 512:(b + 1) * 512], bank(4 + b), ACT.Relu, scale=I_DIM ** -0.5)
                        last.then_inc(*act_s.did("C4"))
                    if G == 4:
                        act.wait_ge(pe_s.sem, pe_s.at(l, "C6"))
                        evac(probT[:, 0:512], 4)
                        evac(probT[:, 1024:1536], 6).then_inc(*act_s.did("C6"))
                    if G == 6:
                        act.wait_ge(dve_s.sem, dve_s.at(l, "D2max"))
                        act.activation(ex[:, 0], ex[:, 0], ACT.Exp)
                        softmax(0, D_HEADS, 4, 0, D_DIM ** -0.5).then_inc(*act_s.did("D2"))
                    if G == 8:
                        act.wait_ge(pe_s.sem, pe_s.at(l, "D5"))
                        for b in range(2):
                            last = evac(probT[:, b * 512:(b + 1) * 512], 4 + b)
                        last.then_inc(*act_s.did("D5"))
                    if G == GATES - 1:
                        for i in range(4):
                            turned_hi(l, "M0", 4 + i, lhs[:, 0, 2 * i:2 * i + 2].rearrange("p k s -> p (k s)"), last=(i == 3))
                j = OUT0
                act.wait_ge(mm_done, l * CHUNKS + (j - 3) + 1 + SLOTS)
                act.wait_ge(dve_drained, l * DRAINS + DR_OUT - 1 + PAIRS)
                for t in range(TT):
                    last = act.activation(gate[:, t], bank(t), ACT.Tanh, scale=rn_half[:, t:t + 1])
                last.then_inc(act_drained, 1)
                splits(l, j, j + 2)
                for i in range(2):
                    turned_hi(l, "M1", 4 + i, lhs[:, 0, 8 + 2 * i:10 + 2 * i].rearrange("p k s -> p (k s)"), last=(i == 1))
                splits(l, j + 2, j + 5)
                for i in range(2):
                    turned_hi(l, "M2", 6 + i, lhs[:, 0, 12 + 2 * i:14 + 2 * i].rearrange("p k s -> p (k s)"), last=(i == 1))
                splits(l, j + 5, j + 8)

                def out_squares(n):
                    act.wait_ge(mm_done, l * CHUNKS + OUT0 + (n + 1) * CPG + SLOTS)
                    b0 = (n % 2) * 2
                    act.activation(gate[:, 0], bank(b0), ACT.Square, accum_out=sq[:, 0, n:n + 1]).then_inc(*act_s.did(f"sq{n}0"))
                    act.wait_ge(dve_s.sem, dve_s.at(l, f"og{n}"))
                    act.activation(gate[:, 1], bank(b0 + 1), ACT.Square, accum_out=sq[:, 1, n:n + 1]).then_inc(*act_s.did(f"sq{n}1"))

                for n in range(1, NG):
                    j = OUT0 + n * CPG
                    splits(l, j, j + 4)
                    out_squares(n - 1)
                    splits(l, j + 4, j + 8)
                act.wait_ge(pe_s.sem, pe_s.at(l, "out3"))
                act.activation(gate[:, 0], bank(2), ACT.Square, accum_out=sq[:, 0, 3:4]).then_inc(*act_s.did("sq30"))
                act.wait_ge(mm_done, (l + 1) * CHUNKS + SLOTS)
                act.activation(gate[:, 1], bank(3), ACT.Square, accum_out=sq[:, 1, 3:4]).then_inc(*act_s.did("sq31"))
                assert act_s.n == len(ACT_STEPS)

        @block.vector
        def _(dve):
            links = [0]
            DVE_LINKS = 135

            def link(ins):
                links[0] += 1
                ins.then_inc(dve_link, 1)
                dve.wait_ge(dve_link, l * DVE_LINKS + links[0])

            def own_wait():
                dve.sem_inc(dve_waited, 1)

            def split(l, j, jn=None):
                jn = j if jn is None else jn
                n, s = w_width(jn), jn % SLOTS
                dve.wait_ge(hi_done, l * CHUNKS + j + 1)
                dve.tensor_tensor(wslot(w_lo, s, n), wslot(raw, s, n), wslot(w_hi, s, n).bitcast(F32),
                                  ALU.subtract).then_inc(lo_done, 1)

            def splits(l, a, b):
                for j in range(a, b):
                    split(l, j)

            def drain(l, q, dst, seen, scale=1.0):
                dve.wait_ge(mm_done, l * CHUNKS + seen + 1 + SLOTS)
                dve.tensor_scalar(dst, bank((q % 2) * 2 + 1, 0, dst.shape[-1]), scale, None, ALU.mult).then_inc(dve_drained, 1)

            def rsqrt(n):
                v, y, a, m = ms[:, 0:n], rs[:, 0:n], nt[:, 0:n], mh[:, 0:n]
                dve.tensor_scalar(m, v, -0.5, None, ALU.mult)
                link(dve.tensor_scalar(half[:, 0:n], v.bitcast(I32), 1, None, ALU.logical_shift_right))
                link(dve.tensor_scalar(y.bitcast(I32), half[:, 0:n], -1.0, float(0x5f3759df), ALU.mult, ALU.add))
                for i in range(3):
                    for c in range(n):
                        yc = y[:, c:c + 1]
                        last = dve.scalar_tensor_tensor(out=a[:, c:c + 1], in0=yc, scalar=yc, in1=m[:, c:c + 1],
                                                        op0=ALU.mult, op1=ALU.mult)
                    link(last)
                    last = dve.scalar_tensor_tensor(out=y, in0=a, scalar=1.5, in1=y, op0=ALU.add, op1=ALU.mult)
                    if i < 2:
                        link(last)
                return last

            def mean_square(dst, v, n):
                return dve.tensor_tensor_reduce(gate[:, 0, 0:n], v, v, 1.0 / n, EPS,
                                                ALU.mult, ALU.add, dst)

            def turned_lo(l, name, b, dst, hi, scale=1.0, last=True):
                ins = dve.scalar_tensor_tensor(out=dst, in0=bank(b), scalar=scale, in1=hi.bitcast(F32),
                                               op0=ALU.mult, op1=ALU.subtract)
                if last:
                    ins.then_inc(*dve_s.did(name))

            def both(buf, i, k):
                return (buf[:, i, k:k + 2].rearrange("p k s -> p (k s)"))

            def y_turned(name, buf, scale):
                dve.wait_ge(act_s.sem, act_s.at(l, name))
                for i in range(2):
                    turned_lo(l, name, 4 + i, both(yT[:, buf], 1, 2 * i), both(yT[:, buf], 0, 2 * i), scale, last=(i == 1))

            def times_silu(name, part_name):
                dve.wait_ge(act_s.sem, act_s.at(l, name))
                z = part(part_name, BW)
                dve.scalar_tensor_tensor(out=z, in0=gate[:], scalar=1.0, in1=z, op0=ALU.add, op1=ALU.mult).then_inc(*dve_s.did(name))

            def zero_others(tiles):
                for r in range(2):
                    dve.memset(tiles[(1 - r) * 64:(2 - r) * 64, r], 0.0)

            def row_max(l, t, heads, width, b0):
                per = 512 // width
                for b in range(heads // per):
                    last = dve.tensor_reduce(mx[:, t, b * per:(b + 1) * per],
                                             bank(b0 + b).rearrange("p (h s) -> p h s", h=per), AX_X, ALU.max)
                return last

            def attended(name, dst, z, b0, heads, ts):
                dve.wait_ge(pe_s.sem, pe_s.at(l, name))
                for i, t in enumerate(ts):
                    r = rinv[:, t, 0:heads].unsqueeze(2).to_broadcast([P, heads, BW // heads])
                    link(dve.tensor_tensor(dst[:, t].rearrange("p (h d) -> p h d", h=heads),
                                           bank(b0 + i).rearrange("p (h d) -> p h d", h=heads), r, ALU.mult))
                    last = dve.tensor_tensor(dst[:, t], dst[:, t], z[:, t], ALU.mult)
                last.then_inc(*dve_s.did(name))

            rn_of_tile = rn[:, 1:2]

            def col(g):
                return proj[:, 1, g * MW:(g + 1) * MW]

            def residual(n, part=0, parts=1, each=None):
                w = NW // parts
                c = slice(n * NW + part * w, n * NW + (part + 1) * w)
                for t in range(TT):
                    last = dve.scalar_tensor_tensor(out=wide[:, t, c], in0=wide[:, t, c], scalar=rs[:, t:t + 1], in1=area[:, t, c],
                                                    op0=ALU.mult, op1=ALU.add)
                    if each is not None:
                        last.then_inc(each, 1)
                return last

            dve.memset(top[:], 0.0).then_inc(mm_done, SLOTS)
            dve.memset(rs[:], 0.0)
            dve.memset(wide[:, 1], 0.0).then_inc(wide_cleared, 1)
            dve.wait_ge(wide_cleared, 2)

            def stream_head(count):
                dve.wait_ge(res_loaded[0], count)
                for i in range(2):
                    residual(0, i, 2).then_inc(head_ready, 1)
            stream_head(16)
            dve.wait_ge(gcols_turned, 1)
            dve.tensor_copy(gcols[:], bank(0, 0, 40)).then_inc(gcols_turned, 1)

            with nc.vector.Fori(0, DEPTH, 1) as l:
                def stream(n):
                    dve.wait_ge(res_loaded[n], l * 16 + 16)
                    residual(n).then_inc(*dve_s.did(f"xn{n}"))

                def input_lo(b):
                    dve.wait_ge(act_s.sem, act_s.at(l, f"hT{b}"))
                    for i in range(2):
                        k = 2 * b + i
                        last = dve.scalar_tensor_tensor(out=lhs[:, 1, k], in0=bank(4 + b % 4, i * SEQ, SEQ), scalar=gcol[:, k:k + 1],
                                                        in1=lhs[:, 0, k].bitcast(F32), op0=ALU.mult, op1=ALU.subtract)
                    last.then_inc(*dve_s.did(f"hT{b}"))

                input_lo(0)
                input_lo(1)
                stream(1)
                dve.wait_ge(lo_done, l * CHUNKS + 1 + SLOTS)
                splits(l, 1, 3)
                input_lo(2)
                input_lo(3)
                stream(2)
                splits(l, 3, 5)
                input_lo(4)
                input_lo(5)
                dve.wait_ge(dve_drained, l * DRAINS + PAIRS)
                stream(3)
                splits(l, 5, 7)
                input_lo(6)
                input_lo(7)
                splits(l, 7, 8)
                dve.wait_ge(pool_s.sem, pool_s.at(l, "mask"))
                dve.wait_ge(act_s.sem, act_s.at(l, "ss"))
                link(dve.tensor_reduce(ms[:, 0:TT], ss[:], AX_X, ALU.add))
                link(dve.tensor_scalar(ms[:, 0:TT], ms[:, 0:TT], 1.0 / D_MODEL, EPS, ALU.mult, ALU.add))
                link(rsqrt(TT))
                dve.tensor_scalar(rn_half[:], rs[:, 0:TT], 0.5, None, ALU.mult)
                dve.tensor_copy(rn[:], rs[:, 0:TT]).then_inc(*dve_s.did("rn"))
                with nc.vector.Fori(0, 2, 1) as i:
                    for h in range(2):
                        j0 = (1 + h) * CPG
                        for c in range(4):
                            split(l, i * (2 * CPG) + (j0 + c), j0 + c)
                        dve.wait_ge(dve_s.sem, dve_s.at(l, "rn"))
                        dve.wait_ge(mm_done, (l * CHUNKS + (j0 + SLOTS)) + i * (2 * CPG))
                        dve.tensor_scalar(proj[:, 1, bass.ds(i * (2 * MW) + h * MW, MW)], bank(h * 2 + 1, 0, MW), rn[:, 1:2], None,
                                          ALU.mult).then_inc(dve_drained, 1)
                        for c in range(4, CPG):
                            split(l, i * (2 * CPG) + (j0 + c), j0 + c)
                j = 5 * CPG
                splits(l, j, j + 4)
                drain(l, 4, col(4), j - 1, rn_of_tile)
                splits(l, j + 4, j + 5)
                dve.wait_ge(pe_s.sem, pe_s.at(l, "A1"))
                wt = bank(4).rearrange("p (g s) -> p g s", g=A_GROUPS)
                dve.tensor_copy(a_wT[0:64], wt[0:64])
                dve.memset(a_wT[64:128, :, 0:64], 0.0)
                dve.tensor_copy(a_wT[64:128, :, 64:128], wt[64:128, :, 64:128]).then_inc(*dve_s.did("A1"))
                splits(l, j + 5, j + 8)
                j = 6 * CPG
                splits(l, j, j + 1)
                dve.wait_ge(act_s.sem, act_s.at(l, "gelu"))
                u, v = part("a_u", BW), part("a_v", BW)
                dve.scalar_tensor_tensor(out=u, in0=gelu_arg[:, :, 0:BW], scalar=1.0, in1=u, op0=ALU.add, op1=ALU.mult)
                link(dve.scalar_tensor_tensor(out=v, in0=gelu_arg[:, :, BW:2 * BW], scalar=1.0, in1=v, op0=ALU.add, op1=ALU.mult))
                for t in range(TT):
                    last = dve.bn_stats(bn[:, t], v[:, t])
                last.then_inc(*dve_s.did("gelu"))
                splits(l, j + 1, j + 4)
                drain(l, 5, col(5), j - 1, rn_of_tile)
                splits(l, j + 4, j + 5)
                dve.wait_ge(dve_s.sem, dve_s.at(l, "gelu"))
                own_wait()
                for t in range(TT):
                    last = dve.bn_aggr(mv[:, t], bn[:, t])
                link(last)
                link(dve.tensor_scalar(ms[:, 0:2], mv[:, :, 1], 0.25, EPS, ALU.mult, ALU.add))
                link(rsqrt(2))
                link(dve.tensor_scalar(rs[:, 0:2], rs[:, 0:2], 0.5, None, ALU.mult))
                for t in range(TT):
                    last = dve.tensor_scalar(v[:, t], v[:, t], mv[:, t, 0:1], rs[:, t:t + 1], ALU.subtract, ALU.mult)
                link(last)
                dve.wait_ge(gains_loaded, l * 80 + 80)
                dve.tensor_tensor(v, v, g_ln.unsqueeze(1).to_broadcast([P, TT, BW]), ALU.mult).then_inc(*dve_s.did("vn"))
                splits(l, j + 5, j + 8)
                times_silu("zA", "a_z")
                j = 7 * CPG
                splits(l, j, j + 1)
                dve.wait_ge(dve_s.sem, dve_s.at(l, "zA"))
                cq, ckv = part("b_cq", BW), part("b_ckv", B_KV_RANK)
                dve.wait_ge(act_drained, l * DR_OUT + 5 + PAIRS)
                for t in range(TT):
                    link(mean_square(ms[:, t:t + 1], cq[:, t], B_Q_RANK))
                    link(mean_square(ms[:, 2 + t:3 + t], ckv[:, t], B_KV_RANK))
                link(rsqrt(4))
                for t in range(TT):
                    dve.scalar_tensor_tensor(out=cq[:, t], in0=cq[:, t], scalar=rs[:, t:t + 1], in1=g_q, op0=ALU.mult, op1=ALU.mult)
                    last = dve.scalar_tensor_tensor(out=ckv[:, t], in0=ckv[:, t], scalar=rs[:, 2 + t:3 + t], in1=g_kv, op0=ALU.mult, op1=ALU.mult)
                last.then_inc(*dve_s.did("Bn"))
                splits(l, j + 1, j + 4)
                drain(l, 6, col(6), j - 1, rn_of_tile)
                splits(l, j + 4, j + 5)
                dve.wait_ge(pe_s.sem, pe_s.at(l, "A2"))
                bb = bcol[:].unsqueeze(2).to_broadcast([P, A_GROUPS, P])
                for t in range(TT):
                    link(dve.tensor_tensor(v[:, t].rearrange("p (g s) -> p g s", g=A_GROUPS),
                                           bank(4 + t).rearrange("p (g s) -> p g s", g=A_GROUPS), bb, ALU.add))
                link(dve.tensor_tensor(u, u, v, ALU.mult))
                dve.tensor_tensor(u, u, part("a_z", BW), ALU.mult).then_inc(*dve_s.did("A2"))
                splits(l, j + 5, j + 8)
                j = 8 * CPG
                splits(l, j, j + 4)
                drain(l, 7, col(7), j - 1, rn_of_tile)
                splits(l, j + 4, j + 5)
                dve.wait_ge(act_s.sem, act_s.at(l, "B1"))
                turned_lo(l, "B1", 6, both(yT[:, 0], 1, 0), both(yT[:, 0], 0, 0), last=False)
                turned_lo(l, "B1", 7, both(yT[:, 0], 1, 2), both(yT[:, 0], 0, 2), last=False)
                turned_lo(l, "B1", 4, both(yT[:, 1], 1, 0), both(yT[:, 1], 0, 0))
                splits(l, j + 5, j + 8)
                j = LATENT0
                n = B_HEADS * QW // 2
                splits(l, j, j + 4)
                drain(l, 8, col(8), j - 1, rn_of_tile)
                splits(l, j + 4, j + 6)
                drain(l, 9, lat_q[:, 1, 0:n], j + 1)
                splits(l, j + 6, j + 8)
                drain(l, 10, lat_q[:, 1, n:2 * n], j + 3)
                j = LATENT0 + LATENT
                splits(l, j, j + 2)
                drain(l, 11, lat_kv[:, 1, 0:512], j - 3)
                splits(l, j + 2, j + 4)
                drain(l, 12, lat_kv[:, 1, 512:1024], j - 1)
                splits(l, j + 4, j + 5)
                y_turned("yA", 0, 0.125)
                splits(l, j + 5, j + 8)
                times_silu("zB", "b_z")
                j += CPG
                splits(l, j, j + 4)
                drain(l, 13, col(9), j - 1, rn_of_tile)
                splits(l, j + 4, j + 5)
                dve.wait_ge(pe_s.sem, pe_s.at(l, "B3k"))
                zero_others(krT)
                dve.tensor_copy(knT[:, 2:4].rearrange("p k s -> p (k s)"), bank(7)).then_inc(*dve_s.did("B3k"))
                splits(l, j + 5, j + 8)
                dve.wait_ge(act_drained, l * DR_OUT + 13 + PAIRS)
                ik = part("c_ik", I_DIM)
                for t in range(TT):
                    last = dve.bn_stats(bn[:, t], ik[:, t])
                link(last)
                own_wait()
                for t in range(TT):
                    last = dve.bn_aggr(mv[:, t], bn[:, t])
                link(last)
                link(dve.tensor_scalar(ms[:, 0:2], mv[:, :, 1], EPS, None, ALU.add))
                link(rsqrt(2))
                for t in range(TT):
                    last = dve.tensor_scalar(ik[:, t], ik[:, t], mv[:, t, 0:1], rs[:, t:t + 1], ALU.subtract, ALU.mult)
                link(last)
                dve.tensor_scalar(iw[:], part("c_iw", I_HEADS), I_HEADS ** -0.5, None, ALU.mult)
                dve.tensor_tensor(ik, ik, g_ik.unsqueeze(1).to_broadcast([P, TT, I_DIM]), ALU.mult).then_inc(*dve_s.did("ikn"))
                j += CPG
                splits(l, j, j + 1)
                dve.wait_ge(pe_s.sem, pe_s.at(l, "B3q"))
                dve.tensor_copy(qnT[:, 2:4].rearrange("p k s -> p (k s)"), bank(6)).then_inc(*dve_s.did("B3q"))
                splits(l, j + 1, j + 4)
                drain(l, 14, col(10), j - 1, rn_of_tile)
                splits(l, j + 4, j + 5)

                def maxima(name, out_name, b0s, heads, ts, scale):
                    dve.wait_ge(pe_s.sem, pe_s.at(l, name))
                    for t in ts:
                        last = row_max(l, t, heads, 128 * (t + 1), b0s[t])
                    link(last)
                    a, b = ts[0], ts[-1] + 1
                    dve.tensor_scalar(nmx[:, a:b, 0:heads], mx[:, a:b, 0:heads], -scale, None, ALU.mult).then_inc(*dve_s.did(out_name))

                maxima("B4", "B4max", (4, 5), B_HEADS, (0, 1), QW ** -0.5)
                splits(l, j + 5, j + 8)

                def sink_maxima(name, out_name, t):
                    dve.wait_ge(pe_s.sem, pe_s.at(l, name))
                    link(row_max(l, t, D_HEADS, 128 * (t + 1), 4))
                    link(dve.scalar_tensor_tensor(out=mx[:, t], in0=mx[:, t], scalar=D_DIM ** -0.5, in1=sink, op0=ALU.mult, op1=ALU.max))
                    dve.tensor_tensor(ex[:, t], sink, mx[:, t], ALU.subtract)
                    dve.tensor_scalar(nmx[:, t], mx[:, t], -1.0, None, ALU.mult).then_inc(*dve_s.did(out_name))

                def index_score(name, t):
                    width = 128 * (t + 1)
                    dve.wait_ge(act_s.sem, act_s.at(l, name))
                    for h in range(I_HEADS):
                        prev = mask[:, 1, SEQ - width:SEQ] if h == 0 else idx_score[:, t, 0:width]
                        last = dve.scalar_tensor_tensor(out=idx_score[:, t, 0:width], in0=probT[:, h * width:(h + 1) * width],
                                                        scalar=iw[:, t, h:h + 1], in1=prev, op0=ALU.mult, op1=ALU.add)
                        if h < I_HEADS - 1:
                            link(last)
                    last.then_inc(*dve_s.did(name))
                    dve.wait_ge(dve_s.sem, dve_s.at(l, name))

                def select(name, t, r0, r1):
                    width = 128 * (t + 1)
                    first, dst = idx_score[:, t, 0:width], idx_work[:, t, 0:width]
                    for r in range(r0, r1):
                        src = dst if r else first
                        own_wait()
                        link(dve.max(top[:], src))
                        own_wait()
                        link(dve.match_replace(dst, top[:], src, TAKEN))
                    if r1 == N_SEL // 8:
                        link(dve.tensor_scalar(dst, dst, TAKEN, None, ALU.not_equal))
                        dve.tensor_scalar(sel[:, t, 0:width], dst, NEG, None, ALU.mult).then_inc(*dve_s.did(name))

                def merge(G, ahead=lambda: None):
                    b, n = G // NG, G % NG
                    dve.wait_ge(act_drained, l * DR_OUT + DR_GATE + G + 1 + PAIRS)
                    dve.wait_ge(mm_done, l * CHUNKS + GATE0 + (G + 1) * CG + SLOTS)
                    cols = wide[:, :, n * NW:(n + 1) * NW]
                    for t in range(TT):
                        dst = cols[:, t] if b == 0 else gate[:, t]
                        last = dve.scalar_tensor_tensor(out=dst, in0=gate[:, t], scalar=1.0, in1=bank(2 + t), op0=ALU.add, op1=ALU.mult)
                    if b > 0:
                        link(last)
                        ahead()
                        last = dve.tensor_tensor(cols, cols, gate[:], ALU.add)
                    last.then_inc(dve_drained, 1)

                for G in range(GATES):
                    j = GATE0 + G * CG
                    splits(l, j, j + 1)
                    if G == 3:
                        select("sel1", 1, 0, 3)
                    if G == 0:
                        dve.wait_ge(act_s.sem, act_s.at(l, "B4"))
                        dve.reciprocal(rinv[:, :, 0:4], sums[:, :, 0:4])
                        dve.wait_ge(pe_s.sem, pe_s.at(l, "B5"))
                        dve.tensor_copy(probT[:, 512:1024], bank(5)).then_inc(*dve_s.did("B5"))
                    splits(l, j + 1, j + 4)
                    if G == 0:
                        drain(l, 15, col(11), j - 1, rn_of_tile)
                    else:
                        merge(G - 1)
                    splits(l, j + 4, j + 5)
                    if G == 0:
                        dve.wait_ge(dve_s.sem, dve_s.at(l, "B5"))
                        attended("B6", part("b_cq", BW), part("b_z", BW), 4, B_HEADS, (0, 1))
                    if G == 1:
                        dve.wait_ge(pe_s.sem, pe_s.at(l, "C1"))
                        zero_others(cikT)
                        dve.tensor_copy(cqT[:, 2:4].rearrange("p k s -> p (k s)"), bank(5))
                        dve.tensor_copy(ciqT[:, 2:4].rearrange("p k s -> p (k s)"), bank(7)).then_inc(*dve_s.did("C1"))
                    if G == 2:
                        index_score("C3", 0)
                    if G == 3:
                        select("sel1", 1, 3, 6)
                    if G == 4:
                        maxima("C5", "C5max", (4, 5), C_HEADS, (0, 1), C_DIM ** -0.5)
                    if G == 5:
                        attended("C7", part("c_q", BW), part("c_z", BW), 4, C_HEADS, (0, 1))
                    if G == 6:
                        dve.wait_ge(pe_s.sem, pe_s.at(l, "D1"))
                        dve.tensor_copy(dqT[:, 2:4].rearrange("p k s -> p (k s)"), bank(5))
                        by_row = dkT.rearrange("p (j r) s -> p r j s", r=2)
                        zero_others(by_row)
                        for r in range(2):
                            last = dve.tensor_copy(by_row[r * 64:(r + 1) * 64, r],
                                                   ps[r * 64:(r + 1) * 64, 6].rearrange("p (j s) -> p j s", j=D_KV))
                        last.then_inc(*dve_s.did("D1"))
                    if G == 7:
                        dve.wait_ge(act_s.sem, act_s.at(l, "D2"))
                        link(dve.tensor_tensor(sums[:, 0], sums[:, 0], ex[:, 0], ALU.add))
                        dve.reciprocal(rinv[:, 0], sums[:, 0])
                        dve.wait_ge(pe_s.sem, pe_s.at(l, "D4"))
                        dve.tensor_copy(probT[:, 512:1024], bank(5)).then_inc(*dve_s.did("D4"))
                    if G == 8:
                        sink_maxima("D3", "D3max", 1)
                    if G == 9:
                        attended("D6b", part("d_q", BW), part("d_z", BW), 4, D_HEADS, (1,))
                    splits(l, j + 5, j + 8)
                    if G == 0:
                        times_silu("zC", "c_z")
                    if G == 2:
                        select("sel0", 0, 0, 8)
                    if G == 3:
                        select("sel1", 1, 6, 8)
                    splits(l, j + 8, j + 10)
                    if G in (0, 5, 9):
                        y_turned({0: "yB", 5: "yC", 9: "yD"}[G], {0: 1, 5: 0, 9: 1}[G], 0.25)
                    if G == 0:
                        times_silu("zD", "d_z")
                    if G == 2:
                        index_score("C4", 1)
                    if G == 4:
                        dve.wait_ge(act_s.sem, act_s.at(l, "C5"))
                        dve.reciprocal(rinv[:, :, 0:4], sums[:, :, 0:4])
                        dve.wait_ge(pe_s.sem, pe_s.at(l, "C6"))
                        dve.tensor_copy(probT[:, 512:1024], bank(5)).then_inc(*dve_s.did("C6"))
                        dve.wait_ge(dve_s.sem, dve_s.at(l, "C6"))
                    if G == 6:
                        sink_maxima("D2", "D2max", 0)
                    if G == 7:
                        dve.wait_ge(dve_s.sem, dve_s.at(l, "D4"))
                        attended("D6a", part("d_q", BW), part("d_z", BW), 6, D_HEADS, (0,))
                    if G == 8:
                        dve.wait_ge(act_s.sem, act_s.at(l, "D3"))
                        link(dve.tensor_tensor(sums[:, 1], sums[:, 1], ex[:, 1], ALU.add))
                        dve.reciprocal(rinv[:, 1], sums[:, 1])
                        dve.wait_ge(pe_s.sem, pe_s.at(l, "D5"))
                        for b in range(2, 4):
                            last = dve.tensor_copy(probT[:, b * 512:(b + 1) * 512], bank(4 + b))
                        last.then_inc(*dve_s.did("D5"))
                        dve.wait_ge(dve_s.sem, dve_s.at(l, "D5"))
                    if G == GATES - 1:
                        dve.wait_ge(act_s.sem, act_s.at(l, "M0"))
                        for i in range(4):
                            turned_lo(l, "M0", 4 + i, both(lhs, 1, 2 * i), both(lhs, 0, 2 * i), last=(i == 3))
                j = OUT0
                splits(l, j, j + 2)
                merge(GATES - 1, lambda: splits(l, j + 2, j + 3))
                dve.wait_ge(act_s.sem, act_s.at(l, "M1"))
                for i in range(2):
                    turned_lo(l, "M1", 4 + i, both(lhs, 1, 8 + 2 * i), both(lhs, 0, 8 + 2 * i), last=(i == 1))
                splits(l, j + 3, j + 5)
                dve.wait_ge(act_s.sem, act_s.at(l, "M2"))
                for i in range(2):
                    turned_lo(l, "M2", 6 + i, both(lhs, 1, 12 + 2 * i), both(lhs, 0, 12 + 2 * i), last=(i == 1))
                splits(l, j + 5, j + 8)

                def out_drain(n):
                    dve.wait_ge(mm_done, l * CHUNKS + OUT0 + (n + 1) * CPG + SLOTS)
                    dve.wait_ge(post_loaded, l * 16 + 16)
                    c, b0 = slice(n * NW, (n + 1) * NW), (n % 2) * 2
                    dve.tensor_tensor(wide[:, 1, c], bank(b0 + 1), post_g[:, c], ALU.mult).then_inc(*dve_s.did(f"og{n}"))
                    dve.wait_ge(act_s.sem, act_s.at(l, f"sq{n}0"))
                    dve.tensor_tensor(wide[:, 0, c], bank(b0), post_g[:, c], ALU.mult).then_inc(dve_drained, 1)

                for n in range(1, NG):
                    j = OUT0 + n * CPG
                    splits(l, j, j + 4)
                    out_drain(n - 1)
                    splits(l, j + 4, j + 8)
                def last_group(t):
                    return dve.tensor_tensor(wide[:, t, 3 * NW:], bank(2 + t), post_g[:, 3 * NW:], ALU.mult)
                dve.wait_ge(act_s.sem, act_s.at(l, "sq30"))
                last_group(0)
                link(dve.tensor_reduce(ms[:, 0:TT], sq[:, :, 0:NG - 1], AX_X, ALU.add))
                link(dve.tensor_scalar(ms[:, 0:TT], ms[:, 0:TT], 1.0 / D_MODEL, EPS, ALU.mult, ALU.add))
                dve.wait_ge(act_s.sem, act_s.at(l, "sq31"))
                link(dve.scalar_tensor_tensor(out=ms[:, 0:TT], in0=sq[:, :, NG - 1], scalar=1.0 / D_MODEL, in1=ms[:, 0:TT],
                                              op0=ALU.mult, op1=ALU.add))
                link(rsqrt(TT))
                stream_head(l * 16 + 32)
                last_group(1).then_inc(dve_drained, 1)
                assert dve_s.n == len(DVE_STEPS)
            assert links[0] == DVE_LINKS, links[0]
            for n in range(1, NG):
                if n == NG - 1:
                    dve.wait_ge(dve_drained, DEPTH * DRAINS + PAIRS)
                dve.wait_ge(res_loaded[n], DEPTH * 16 + 16)
                residual(n, each=out_ready)

        @block.tensor
        def _(pe):
            def chunk(l, j, jn, left, k0, nk, n, b0, first, last):
                s = jn % SLOTS
                pe.wait_ge(lo_done, l * CHUNKS + j + 1 + SLOTS)
                wh = wslot(w_hi, s, nk * n).rearrange("p (k n) -> p k n", k=nk)
                wl = wslot(w_lo, s, nk * n).rearrange("p (k n) -> p k n", k=nk)
                for k in range(nk):
                    for t in range(TT):
                        hi, lo = (left[:, i, k0 + k, t * P:(t + 1) * P] for i in range(2))
                        o = bank(b0 + t, 0, n)
                        a, z = first and k == 0, last and k == nk - 1
                        pe.matmul(o, hi, wh[:, k], start=a, stop=False)
                        pe.matmul(o, hi, wl[:, k], start=False, stop=False)
                        mm = pe.matmul(o, lo, wh[:, k], start=False, stop=z)
                mm.then_inc(mm_done, 1)

            def chunks(l, j0, left, n, b0, a, b, total=CPG):
                for c in range(a, b):
                    chunk(l, j0 + c, j0 + c, left, KC * c, KC, n, b0, c == 0, c == total - 1)

            def pair_free(l, q):
                pe.wait_ge(act_drained, l * DR_OUT + q + 1 + PAIRS)
                pe.wait_ge(dve_drained, l * DRAINS + q + 1 + PAIRS)

            def turn(b, col, src):
                n = src.shape[-1]
                return pe.transpose(ps[0:n, b, col:col + P], src, ident)

            def turn_y(name, src, b0=4):
                for k in range(BKT):
                    for t in range(TT):
                        last = turn(b0 + k // 2, (k % 2) * SEQ + t * P, src[:, t, k * P:(k + 1) * P])
                last.then_inc(*pe_s.did(name))

            def turn_heads(b0, src, n):
                for k in range(n):
                    for t in range(TT):
                        last = turn(b0 + k // 2, (k % 2) * SEQ + t * P, src[:, t, k * P:(k + 1) * P])
                return last

            def seen(step, name):
                pe.wait_ge(step.sem, step.at(l, name))

            def scores(t, heads, b0, m, qk):
                width = 128 * (t + 1)
                per = 512 // width
                for h in range(heads):
                    b = b0 + h // per
                    if h % per == 0:
                        pe.matmul(bank(b), identb, m.unsqueeze(1).to_broadcast([P, per, width]), start=True, stop=True)
                    pairs = qk(h, width)
                    for i, (q, k) in enumerate(pairs):
                        mm = pe.matmul(bank(b, (h % per) * width, width), q, k, start=False,
                                       stop=True, skip_group_check=True)
                return mm

            def turn_prob(t, heads, b0, at):
                width = 128 * (t + 1)
                i = 0
                for h in range(heads):
                    for k in range(t + 1):
                        last = turn(b0 + i // 4, (i % 4) * P, prob[:, at + h * width + k * P:at + h * width + (k + 1) * P])
                        i += 1
                return last

            def weigh(t, heads, b, at, d, value):
                for h in range(heads):
                    for k in range(t + 1):
                        i = h * (t + 1) + k
                        mm = pe.matmul(bank(b, h * d, d), probT[:, at + i * P:at + (i + 1) * P], value(k, h),
                                       start=(k == 0), stop=(k == t))
                return mm

            def keep_clock(n):
                for i in range(n):
                    pe.matmul(bank(7), ident, tabs[:], start=True, stop=True)

            pe.wait_ge(consts_loaded, 48)
            pe.transpose(ps[:, 0, 0:40], gain_rows, tabs[0:40, 0:40]).then_inc(gcols_turned, 1)
            pe.wait_ge(gcols_turned, 2)
            with nc.tensor.Fori(0, DEPTH, 1) as l:
                for c in range(CPG):
                    if c in (0, 1, 3, 5):
                        n = (c + 1) // 2
                        for b in (2 * n, 2 * n + 1):
                            if n == 0:
                                pe.wait_ge(head_ready, l * 2 + b + 1)
                            else:
                                seen(dve_s, f"xn{n}")
                            if b >= 4:
                                seen(dve_s, f"hT{b - 4}")
                            for i in range(2):
                                for t in range(TT):
                                    k = 2 * b + i
                                    last = turn(4 + b % 4, i * SEQ + t * P, wide[:, t, k * P:(k + 1) * P])
                            last.then_inc(*pe_s.did(f"hT{b}"))
                        if n == 0:
                            keep_clock(1)
                    seen(dve_s, f"hT{c}")
                    chunk(l, c, c, lhs, KC * c, KC, MW, 0, c == 0, c == CPG - 1)
                with nc.tensor.Fori(0, 2, 1) as i:
                    for h in range(2):
                        if h == 1:
                            pe.wait_ge(act_drained, i * 2 + (l * DR_OUT + 1 + PAIRS))
                            pe.wait_ge(dve_drained, i * 2 + (l * DRAINS + 1 + PAIRS))
                        else:
                            pe.wait_ge(act_drained, i * 2 + (l * DR_OUT + PAIRS))
                            pe.wait_ge(dve_drained, i * 2 + (l * DRAINS + PAIRS))
                        for c in range(CPG):
                            chunk(l, i * (2 * CPG) + ((1 + h) * CPG + c), (1 + h) * CPG + c, lhs, KC * c, KC, MW,
                                  2 * ((1 + h) % 2), c == 0, c == CPG - 1)
                for g in range(5, 9):
                    j = g * CPG
                    b0 = 2 * (g % 2)
                    if g == 5:
                        pe.wait_ge(aw_loaded, l * 32 + 32)
                        for i in range(A_GROUPS):
                            last = turn(4, i * P, a_w[:, i // 2, (i % 2) * P:(i % 2 + 1) * P])
                        last.then_inc(*pe_s.did("A1"))
                    if g == 7:
                        seen(dve_s, "vn")
                        for t in range(TT):
                            for i in range(A_GROUPS):
                                mm = pe.matmul(bank(4 + t, i * P, P), a_wT[:, i], part("a_v", BW, t)[:, i * P:(i + 1) * P],
                                               start=True, stop=True)
                        mm.then_inc(*pe_s.did("A2"))
                    if g == 8:
                        seen(dve_s, "Bn")
                        seen(dve_s, "A2")
                        turn_heads(6, part("b_cq", BW), 4)
                        turn_heads(4, part("b_ckv", B_KV_RANK), 2).then_inc(*pe_s.did("B1"))
                    pair_free(l, g - 2)
                    chunks(l, j, lhs, MW, b0, 0, CPG)
                seen(dve_s, "B1")
                j = LATENT0
                for h in range(2):
                    pair_free(l, 7 + h)
                    n = B_HEADS * QW // 2
                    b0 = 2 * ((9 + h) % 2)
                    for c in range(2):
                        chunk(l, j, j, yT[:, 0], KC * c, KC, n, b0, c == 0, c == 1)
                        j += 1
                for h in range(2):
                    pair_free(l, 9 + h)
                    n = B_HEADS * KVW // 2
                    b0 = 2 * ((11 + h) % 2)
                    for c in range(2):
                        chunk(l, j, j, yT[:, 1], c, 1, n, b0, c == 0, c == 1)
                        j += 1
                for g in range(9, MG):
                    j = LATENT0 + LATENT + (g - 9) * CPG
                    q = g + LAT_GROUPS
                    b0 = 2 * (q % 2)
                    if g == 9:
                        turn_y("yA", part("a_u", BW))
                    if g == 10:
                        seen(act_s, "yA")
                        seen(dve_s, "yA")
                        seen(pool_s, "kr")
                        pair_free(l, 12)
                        kv = lat_kv.rearrange("p t (h w) -> p t h w", h=B_HEADS)
                        for h in range(B_HEADS):
                            for t in range(TT):
                                turn(6 + h // 2, (h % 2) * SEQ + t * P, kv[:, t, h, 0:B_NOPE])
                        for t in range(TT):
                            last = turn(4, t * P, kr_twice[:, t])
                        last.then_inc(*pe_s.did("B3k"))
                    if g == 11:
                        seen(act_s, "B3q")
                        seen(dve_s, "B3q")

                        def qk(t):
                            def of_head(h, width):
                                return [(qnT[:, h, t * P:(t + 1) * P], knT[:, h, 0:width]),
                                        (qrT[:, h // 2, t * P:(t + 1) * P], krT[:, h % 2, 0:width])]
                            return of_head
                        scores(0, B_HEADS, 4, mask[:, 1, 128:256], qk(0))
                        scores(1, B_HEADS, 5, mask[:, 1, :], qk(1)).then_inc(*pe_s.did("B4"))
                    pair_free(l, q - 2)
                    chunks(l, j, lhs, MW, b0, 0, 4)
                    if g == 10:
                        seen(act_s, "B3k")
                        seen(dve_s, "B3k")
                        seen(pool_s, "q")
                        qs = lat_q.rearrange("p t (h w) -> p t h w", h=B_HEADS)
                        for h in range(B_HEADS):
                            for t in range(TT):
                                turn(5 + h // 2, (h % 2) * SEQ + t * P, qs[:, t, h, 0:B_NOPE])
                        turn_heads(7, q_rope, 2).then_inc(*pe_s.did("B3q"))
                    if g == 11:
                        seen(act_s, "B4")
                        turn_prob(0, B_HEADS, 4, 0)
                        turn_prob(1, B_HEADS, 5, 512).then_inc(*pe_s.did("B5"))
                    chunks(l, j, lhs, MW, b0, 4, CPG)

                for G in range(GATES):
                    j = GATE0 + G * CG
                    if G == 0:
                        seen(act_s, "B5")
                        seen(dve_s, "B5")
                        kv = lat_kv.rearrange("p t (h w) -> p t h w", h=B_HEADS)
                        weigh(0, B_HEADS, 4, 0, B_V, lambda k, h: kv[:, k, h, B_NOPE:KVW])
                        weigh(1, B_HEADS, 5, 512, B_V, lambda k, h: kv[:, k, h, B_NOPE:KVW]).then_inc(*pe_s.did("B6"))
                    if G == 1:
                        seen(pool_s, "c")
                        seen(act_s, "yB")
                        seen(dve_s, "yB")
                        turn_heads(4, part("c_q", BW), 4)
                        turn_heads(6, part("c_iq", BW), 4).then_inc(*pe_s.did("C1"))
                    if G == 2:
                        seen(act_s, "C2")

                        def index(t):
                            width = 128 * (t + 1)
                            per = 512 // width
                            for h in range(I_HEADS):
                                mm = pe.matmul(bank(4 + h // per, (h % per) * width, width), ciqT[:, h // 2, t * P:(t + 1) * P],
                                               cikT[:, h % 2, 0:width], start=True, stop=True)
                            return mm
                        index(0).then_inc(*pe_s.did("C3"))
                    if G == 4:
                        seen(dve_s, "sel1")

                        def qk(t):
                            return lambda h, width: [(cqT[:, h, t * P:(t + 1) * P], ckT[:, 0, 0:width])]
                        scores(0, C_HEADS, 4, sel[:, 0, 0:128], qk(0))
                        scores(1, C_HEADS, 5, sel[:, 1, :], qk(1)).then_inc(*pe_s.did("C5"))
                    if G == 5:
                        seen(act_s, "C6")
                        seen(dve_s, "C6")
                        weigh(0, C_HEADS, 4, 0, C_DIM, lambda k, h: part("c_v", C_DIM, k))
                        weigh(1, C_HEADS, 5, 512, C_DIM, lambda k, h: part("c_v", C_DIM, k)).then_inc(*pe_s.did("C7"))
                    if G == 6:
                        seen(pool_s, "d")
                        seen(act_s, "yC")
                        seen(dve_s, "yC")
                        turn_heads(4, part("d_q", BW), 4)
                        turn_heads(6, dk_twice, 2).then_inc(*pe_s.did("D1"))
                    if G == 7:
                        seen(act_s, "D2")
                        turn_prob(0, D_HEADS, 4, 0).then_inc(*pe_s.did("D4"))
                    if G == 8:
                        seen(dve_s, "D6a")

                        def qk(t):
                            def of_head(h, width):
                                return [(dqT[:, h // 2, t * P:(t + 1) * P],
                                         dkT[:, 2 * (h // (D_HEADS // D_KV)) + h % 2, 0:width])]
                            return of_head
                        scores(1, D_HEADS, 4, mask[:, 2, :], qk(1)).then_inc(*pe_s.did("D3"))
                    if G == 9:
                        seen(act_s, "D5")
                        seen(dve_s, "D5")
                        weigh(1, D_HEADS, 4, 0, D_DIM,
                              lambda k, h: part("d_v", 128, k)[:, (h // 4) * 64:(h // 4 + 1) * 64]).then_inc(*pe_s.did("D6b"))
                    if G == 0:
                        pair_free(l, DR_GATE - 2)
                    else:
                        pe.wait_ge(act_drained, l * DR_OUT + DR_GATE + G + PAIRS)
                    chunks(l, j, lhs, NW, 0, 0, 5)
                    if G == 0:
                        seen(dve_s, "B6")
                        turn_y("yB", part("b_cq", BW))
                    if G == 1:
                        seen(act_s, "C1")
                        seen(dve_s, "C1")
                        for t in range(TT):
                            turn(4, t * P, part("c_k", C_DIM, t))
                        for t in range(TT):
                            last = turn(4, SEQ + t * P, ik_twice[:, t])
                        last.then_inc(*pe_s.did("C2"))
                    if G == 2:
                        seen(act_s, "C3")
                        index(1).then_inc(*pe_s.did("C4"))
                    if G == 4:
                        seen(act_s, "C5")
                        turn_prob(0, C_HEADS, 4, 0)
                        turn_prob(1, C_HEADS, 5, 512).then_inc(*pe_s.did("C6"))
                    if G == 5:
                        seen(dve_s, "C7")
                        turn_y("yC", part("c_q", BW))
                    if G == 6:
                        seen(act_s, "D1")
                        seen(dve_s, "D1")

                        def qk(t):
                            def of_head(h, width):
                                return [(dqT[:, h // 2, t * P:(t + 1) * P],
                                         dkT[:, 2 * (h // (D_HEADS // D_KV)) + h % 2, 0:width])]
                            return of_head
                        scores(0, D_HEADS, 4, mask[:, 1, 128:256], qk(0)).then_inc(*pe_s.did("D2"))
                    if G == 7:
                        seen(act_s, "D4")
                        seen(dve_s, "D4")
                        weigh(0, D_HEADS, 6, 0, D_DIM,
                              lambda k, h: part("d_v", 128, k)[:, (h // 4) * 64:(h // 4 + 1) * 64]).then_inc(*pe_s.did("D6a"))
                    if G == 8:
                        seen(act_s, "D3")
                        turn_prob(1, D_HEADS, 4, 0).then_inc(*pe_s.did("D5"))
                    if G == 9:
                        seen(dve_s, "D6b")
                        turn_y("yD", part("d_q", BW))
                    chunks(l, j, lhs, NW, 0, 5, CPG)
                    if G == GATES - 1:
                        turn_heads(4, wide, 8).then_inc(*pe_s.did("M0"))
                    b = G // NG
                    if G % NG == 0:
                        seen(dve_s, ("yA", "yB", "yC", "yD")[b])
                    if G == 0:
                        pair_free(l, DR_GATE - 1)
                    else:
                        pe.wait_ge(dve_drained, l * DRAINS + DR_GATE + G + PAIRS)
                    chunks(l, j + CPG, yT[:, b % 2], NW, 2, 0, CPB, CPB)
                seen(dve_s, "M0")
                turn_heads(4, wide[:, :, 2 * NW:3 * NW], 4).then_inc(*pe_s.did("M1"))
                for n in range(NG):
                    if n == 0:
                        pe.wait_ge(act_drained, l * DR_OUT + DR_OUT + PAIRS)
                    elif n == 1:
                        pe.wait_ge(dve_drained, l * DRAINS + DR_OUT + PAIRS)
                    else:
                        seen(act_s, f"sq{n - 2}1")
                        pe.wait_ge(dve_drained, l * DRAINS + DR_OUT + n - 1 + PAIRS)
                    j = OUT0 + n * CPG
                    b0 = 2 * (n % 2)
                    if n == 0:
                        chunks(l, j, lhs, NW, b0, 0, 3)
                        pe.wait_ge(dve_drained, l * DRAINS + DR_OUT + PAIRS)
                        turn_heads(6, wide[:, :, 3 * NW:4 * NW], 4).then_inc(*pe_s.did("M2"))
                        chunks(l, j, lhs, NW, b0, 3, 4)
                        seen(dve_s, "M1")
                        chunks(l, j, lhs, NW, b0, 4, 6)
                        seen(dve_s, "M2")
                        chunks(l, j, lhs, NW, b0, 6, CPG)
                    elif n < NG - 1:
                        chunks(l, j, lhs, NW, b0, 0, CPG)
                    else:
                        chunks(l, j, lhs, NW, b0, 0, CPG - 1)
                        c = CPG - 1
                        pe.wait_ge(lo_done, (l + 1) * CHUNKS + SLOTS)
                        wh, wl = (wslot(w, (j + c) % SLOTS, KC * NW).rearrange("p (k n) -> p k n", k=KC) for w in (w_hi, w_lo))
                        for t in range(TT):
                            for k in range(KC):
                                hi, lo = (lhs[:, i, KC * c + k, t * P:(t + 1) * P] for i in range(2))
                                pe.matmul(bank(b0 + t), hi, wh[:, k], start=False, stop=False)
                                pe.matmul(bank(b0 + t), hi, wl[:, k], start=False, stop=False)
                                mm = pe.matmul(bank(b0 + t), lo, wh[:, k], start=False, stop=k == KC - 1)
                            mm.then_inc(*(pe_s.did("out3") if t == 0 else (mm_done, 1)))
                keep_clock(4)
                assert pe_s.n == len(PE_STEPS)


def constants():
    f = np.float32
    tab = np.zeros((P, 512), f)
    tab[:, 0:128] = np.eye(P, dtype=f)
    pos = np.arange(SEQ, dtype=f)
    for dim, at in ((64, 128), (128, 256)):
        inv = (f(1.0) / (f(10000.0) ** (np.arange(0, dim, 2, dtype=f) / f(dim)))).astype(f)
        ang = (pos[:, None] * inv[None, :]).astype(f)
        for fn, a in ((np.cos, at), (np.sin, at + TT * dim // 2)):
            tab[:, a:a + TT * dim // 2] = fn(ang).astype(f).reshape(TT, P, dim // 2).transpose(1, 0, 2).reshape(P, -1)
    m = np.zeros((P, 3, SEQ), f)
    m[:, 0, 0:P] = np.eye(P, dtype=f)
    chunk = np.arange(SEQ) // CHUNK
    q, k = chunk[P:][:, None], chunk[None, :]
    m[:, 1] = np.where(k <= q, 0.0, NEG)
    m[:, 2] = np.where((k <= q) & (k >= q - 1), 0.0, NEG)
    return tab, m


_INS = ["x", "pre_norm_g", "w_in", "a_ln_g", "a_w_s", "a_b_s", "b_q_norm_g", "b_kv_norm_g", "b_w_uq", "b_w_ukv",
        "c_ik_norm_g", "d_sinks", "w_branch", "w_out", "post_norm_g"]


def kernel(**inputs):
    import concourse.bacc as _bacc
    from concourse.bass_utils import run_bass_kernel_spmd as _run

    nc = _bacc.Bacc("TRN2", target_bir_lowering=False, num_devices=1)
    arrays, args = {}, []
    tab, masks = constants()
    for name, a in [(n, np.ascontiguousarray(inputs[n])) for n in _INS] + [("tables", tab), ("masks", masks)]:
        arrays[f"in_{name}_dram"] = a
        args.append(nc.dram_tensor(f"in_{name}_dram", a.shape, mybir.dt.from_np(a.dtype), kind="ExternalInput").ap())
    args.append(nc.dram_tensor("out_0_dram", (1, SEQ, D_MODEL), F32, kind="ExternalOutput").ap())
    trunk(nc, *args)
    r = _run(nc, [arrays], core_ids=[0])
    return r.results[0]["out_0_dram"]
```
